# Optimizing a Trainium2 kernel written in Bass

```python
import jax
import jax.numpy as jnp
from jax import lax
import numpy as np

D_MODEL = 1024
BATCH = 1
SEQ = 512
DEPTH = 1

HEAD_DIM = 64
N_ATT_HEADS = 8
N_RWKV_HEADS = 8
D_ATT = N_ATT_HEADS * HEAD_DIM
D_RWKV = N_RWKV_HEADS * HEAD_DIM
D_MIX = D_ATT + D_RWKV
ROPE_THETA = 500000.0
N_IDX_HEADS = 8
IDX_DIM = 32
TOPK_MAX = 256
Q_BLOCK = 128
D_DECAY_LORA = 32
D_AAA_LORA = 32
D_GATE_LORA = 64
RWKV_GN_EPS = 64e-5
N_EXPERTS = 32
TOP_K_EXPERTS = 4
D_FF_EXPERT = 1024
SWIGLU_LIMIT = 7.0
SWIGLU_ALPHA = 1.702
MOE_BLOCK = 128
RMS_EPS = 1e-6

ATT_COL_SIZES = (D_ATT, D_ATT, D_ATT, N_IDX_HEADS * IDX_DIM, IDX_DIM, N_IDX_HEADS)
RWKV_COL_SIZES = (D_RWKV, D_RWKV, D_RWKV, D_DECAY_LORA, D_AAA_LORA, D_GATE_LORA)
D_ATT_COLS = 3 * D_ATT + N_IDX_HEADS * IDX_DIM + IDX_DIM + N_IDX_HEADS
D_RWKV_COLS = 3 * D_RWKV + D_DECAY_LORA + D_AAA_LORA + D_GATE_LORA
D_IN = D_ATT_COLS + D_RWKV_COLS

kernel_name = "hybrid_dsa_rwkv7_moe_layer"

def _split_cols(z, sizes):
    return jnp.split(z, np.cumsum(sizes)[:-1].tolist(), axis=-1)

def rms_norm(x, w):
    xf = x.astype(jnp.float32)
    y = xf * lax.rsqrt(jnp.mean(xf * xf, axis=-1, keepdims=True) + RMS_EPS)
    return (y * w.astype(jnp.float32)).astype(x.dtype)

def partial_rotary(x, positions):
    d = x.shape[-1]
    rot = d // 4
    half = rot // 2
    inv_freq = ROPE_THETA ** (-jnp.arange(half, dtype=jnp.float32) / half)
    ang = positions.astype(jnp.float32)[..., None] * inv_freq
    ang = ang.reshape(ang.shape[:2] + (1,) * (x.ndim - 3) + (half,))
    cos, sin = jnp.cos(ang), jnp.sin(ang)
    xf = x.astype(jnp.float32)
    x1, x2, rest = xf[..., :half], xf[..., half:rot], xf[..., rot:]
    out = jnp.concatenate([x1 * cos - x2 * sin, x2 * cos + x1 * sin, rest], axis=-1)
    return out.astype(x.dtype)

def dsa_sparse_attention(q, k, v, iq, ik, iw):
    B, T, H, dh = q.shape
    n_sel = min(TOPK_MAX, T // 4)
    nb = T // Q_BLOCK
    idx_scale = (IDX_DIM * N_IDX_HEADS) ** -0.5
    att_scale = HEAD_DIM ** -0.5
    batch_ix = jnp.arange(B)[:, None, None]
    s_pos = jnp.arange(T)

    def to_blocks(a):
        return a.reshape((B, nb, Q_BLOCK) + a.shape[2:]).swapaxes(0, 1)

    def one_block(args):
        qb, iqb, iwb, start = args
        t_pos = start + jnp.arange(Q_BLOCK)
        dots = jnp.einsum("bqhd,bsd->bqhs", iqb, ik, preferred_element_type=jnp.float32)
        score = jnp.einsum("bqh,bqhs->bqs", iwb.astype(jnp.float32), jax.nn.relu(dots)) * idx_scale
        causal = s_pos[None, :] <= t_pos[:, None]
        score = jnp.where(causal[None], score, -jnp.inf)
        _, sel = lax.top_k(score, n_sel)
        valid = sel <= t_pos[None, :, None]
        k_sel = k[batch_ix, sel]
        v_sel = v[batch_ix, sel]
        logits = jnp.einsum("bqhd,bqkhd->bhqk", qb, k_sel, preferred_element_type=jnp.float32) * att_scale
        logits = jnp.where(valid[:, None], logits, -jnp.inf)
        p = jax.nn.softmax(logits, axis=-1)
        return jnp.einsum("bhqk,bqkhd->bqhd", p.astype(v.dtype), v_sel)

    starts = jnp.arange(nb) * Q_BLOCK
    out = lax.map(one_block, (to_blocks(q), to_blocks(iq), to_blocks(iw), starts))
    return out.swapaxes(0, 1).reshape(B, T, H, dh)

def token_shift(z, mu):
    prev = jnp.pad(z, ((0, 0), (1, 0), (0, 0)))[:, :-1]
    return z + (prev - z) * mu

def rwkv7_time_mix(r, k, v, wd, ad, gd, w0, w2, a0, a2, g2, k_k, k_a, r_k, ln_w, ln_b):
    B, T, _ = r.shape
    H, N = N_RWKV_HEADS, HEAD_DIM
    f32 = jnp.float32
    r, k, v, wd, ad, gd = (z.astype(f32) for z in (r, k, v, wd, ad, gd))
    log_w = -jax.nn.softplus(-(w0 + jnp.tanh(wd) @ w2)) - 0.5
    decay = jnp.exp(-jnp.exp(log_w))
    a = jax.nn.sigmoid(a0 + ad @ a2)
    g = jax.nn.sigmoid(gd) @ g2
    kk = (k * k_k).reshape(B, T, H, N)
    kk = kk * lax.rsqrt(jnp.maximum(jnp.sum(kk * kk, axis=-1, keepdims=True), 1e-24))
    k = k * (1.0 + (a - 1.0) * k_a)
    heads = lambda z: z.reshape(B, T, H, N)
    r, decay, k, v, a = heads(r), heads(decay), heads(k), heads(v), heads(a)

    def step(S, inp):
        r_t, w_t, k_t, v_t, kk_t, a_t = inp
        sa = jnp.einsum("bhij,bhj->bhi", S, kk_t)
        S = (S * w_t[:, :, None, :]
             - sa[..., None] * (kk_t * a_t)[:, :, None, :]
             + v_t[..., None] * k_t[:, :, None, :])
        return S, jnp.einsum("bhij,bhj->bhi", S, r_t)

    xs = tuple(z.swapaxes(0, 1) for z in (r, decay, k, v, kk, a))
    _, y = lax.scan(step, jnp.zeros((B, H, N, N), f32), xs)
    y = y.swapaxes(0, 1)
    mean = jnp.mean(y, axis=-1, keepdims=True)
    var = jnp.mean(jnp.square(y - mean), axis=-1, keepdims=True)
    y = ((y - mean) * lax.rsqrt(var + RWKV_GN_EPS)).reshape(B, T, H * N) * ln_w + ln_b
    bonus = jnp.sum(r * k * r_k, axis=-1, keepdims=True) * v
    return (y + bonus.reshape(B, T, H * N)) * g

def moe_ffn(xn, router_w, router_b, w_gu, b_gu, w_dn, b_dn):
    B, T, D = xn.shape
    n_tok = B * T
    xt = xn.reshape(n_tok, D)
    logits = (xt @ router_w + router_b).astype(jnp.float32)
    top_val, top_e = lax.top_k(logits, TOP_K_EXPERTS)
    gates = jax.nn.softmax(top_val, axis=-1)
    n_asg = n_tok * TOP_K_EXPERTS
    flat_e = top_e.reshape(n_asg)
    flat_tok = jnp.arange(n_asg, dtype=jnp.int32) // TOP_K_EXPERTS
    order = jnp.argsort(flat_e)
    se, stok, sg = flat_e[order], flat_tok[order], gates.reshape(n_asg)[order]
    counts = jnp.zeros((N_EXPERTS,), jnp.int32).at[flat_e].add(1)
    padded = (counts + MOE_BLOCK - 1) // MOE_BLOCK * MOE_BLOCK
    start = jnp.cumsum(counts) - counts
    pend = jnp.cumsum(padded)
    pstart = pend - padded
    dest = pstart[se] + (jnp.arange(n_asg, dtype=jnp.int32) - start[se])
    n_rows = (-(-n_asg // MOE_BLOCK) + N_EXPERTS) * MOE_BLOCK
    n_blk = n_rows // MOE_BLOCK
    row_tok = jnp.full((n_rows,), n_tok, jnp.int32).at[dest].set(stok)
    row_g = jnp.zeros((n_rows,), jnp.float32).at[dest].set(sg)
    blk_e = jnp.clip(jnp.searchsorted(pend, jnp.arange(n_blk) * MOE_BLOCK, side="right"), 0, N_EXPERTS - 1)
    x_pad = jnp.concatenate([xt, jnp.zeros((1, D), xt.dtype)], axis=0)
    xb = x_pad[row_tok].reshape(n_blk, MOE_BLOCK, D)

    def expert_block(args):
        xblk, e = args
        hgu = xblk @ w_gu[e] + b_gu[e]
        glu = jnp.minimum(hgu[:, :D_FF_EXPERT], SWIGLU_LIMIT)
        lin = jnp.clip(hgu[:, D_FF_EXPERT:], -SWIGLU_LIMIT, SWIGLU_LIMIT)
        act = (lin + 1.0) * glu * jax.nn.sigmoid(SWIGLU_ALPHA * glu)
        return act @ w_dn[e] + b_dn[e]

    yb = lax.map(expert_block, (xb, blk_e)).reshape(n_rows, D)
    y = jax.ops.segment_sum(yb * row_g[:, None].astype(yb.dtype), row_tok, num_segments=n_tok + 1)[:n_tok]
    return y.reshape(B, T, D)

def setup_inputs(seed: int = 0) -> dict:
    key = jax.random.key(seed)
    ks = jax.random.split(key, 24)
    f32 = jnp.float32
    L = DEPTH

    def nrm(kk, shape, scale):
        return jax.random.normal(kk, shape, f32) * scale

    return {
        "x": nrm(ks[0], (BATCH, SEQ, D_MODEL), 1.0),
        "positions": jnp.tile(jnp.arange(SEQ, dtype=jnp.int32)[None], (BATCH, 1)),
        "norm1_w": 1.0 + nrm(ks[1], (L, D_MODEL), 0.02),
        "w_in": nrm(ks[2], (L, D_MODEL, D_IN), D_MODEL ** -0.5),
        "q_norm_w": 1.0 + nrm(ks[3], (L, HEAD_DIM), 0.02),
        "k_norm_w": 1.0 + nrm(ks[4], (L, HEAD_DIM), 0.02),
        "rwkv_mu": jax.random.uniform(ks[5], (L, D_RWKV_COLS), f32),
        "rwkv_w0": jax.random.uniform(ks[6], (L, D_RWKV), f32, -5.0, 1.0),
        "rwkv_w2": nrm(ks[7], (L, D_DECAY_LORA, D_RWKV), 0.1),
        "rwkv_a0": nrm(ks[8], (L, D_RWKV), 0.1),
        "rwkv_a2": nrm(ks[9], (L, D_AAA_LORA, D_RWKV), D_AAA_LORA ** -0.5),
        "rwkv_g2": nrm(ks[10], (L, D_GATE_LORA, D_RWKV), D_GATE_LORA ** -0.5),
        "rwkv_k_k": 0.85 + nrm(ks[11], (L, D_RWKV), 0.05),
        "rwkv_k_a": 1.0 + nrm(ks[12], (L, D_RWKV), 0.05),
        "rwkv_r_k": nrm(ks[13], (L, N_RWKV_HEADS, HEAD_DIM), 0.1),
        "rwkv_ln_w": 1.0 + nrm(ks[14], (L, D_RWKV), 0.02),
        "rwkv_ln_b": nrm(ks[15], (L, D_RWKV), 0.01),
        "w_out": nrm(ks[16], (L, D_MIX, D_MODEL), D_MIX ** -0.5),
        "norm2_w": 1.0 + nrm(ks[17], (L, D_MODEL), 0.02),
        "router_w": nrm(ks[18], (L, D_MODEL, N_EXPERTS), D_MODEL ** -0.5),
        "router_b": nrm(ks[19], (L, N_EXPERTS), 0.01),
        "exp_w_gu": nrm(ks[20], (L, N_EXPERTS, D_MODEL, 2 * D_FF_EXPERT), D_MODEL ** -0.5),
        "exp_b_gu": nrm(ks[21], (L, N_EXPERTS, 2 * D_FF_EXPERT), 0.01),
        "exp_w_down": nrm(ks[22], (L, N_EXPERTS, D_FF_EXPERT, D_MODEL), D_FF_EXPERT ** -0.5),
        "exp_b_down": nrm(ks[23], (L, N_EXPERTS, D_MODEL), 0.01),
    }

def reference(x, positions, norm1_w, w_in, q_norm_w, k_norm_w, rwkv_mu, rwkv_w0, rwkv_w2,
              rwkv_a0, rwkv_a2, rwkv_g2, rwkv_k_k, rwkv_k_a, rwkv_r_k, rwkv_ln_w, rwkv_ln_b,
              w_out, norm2_w, router_w, router_b, exp_w_gu, exp_b_gu, exp_w_down, exp_b_down):
    B, T, _ = x.shape
    h = x
    for l in range(DEPTH):
        xn = rms_norm(h, norm1_w[l])
        z = xn @ w_in[l]
        att_cols, rw_cols = z[..., :D_ATT_COLS], z[..., D_ATT_COLS:]

        q, k, v, iq, ik, iw = _split_cols(att_cols, ATT_COL_SIZES)
        q = partial_rotary(rms_norm(q.reshape(B, T, N_ATT_HEADS, HEAD_DIM), q_norm_w[l]), positions)
        k = partial_rotary(rms_norm(k.reshape(B, T, N_ATT_HEADS, HEAD_DIM), k_norm_w[l]), positions)
        v = v.reshape(B, T, N_ATT_HEADS, HEAD_DIM)
        iq = partial_rotary(iq.reshape(B, T, N_IDX_HEADS, IDX_DIM), positions)
        ik = partial_rotary(ik, positions)
        att = dsa_sparse_attention(q, k, v, iq, ik, iw).reshape(B, T, D_ATT)

        rw_cols = token_shift(rw_cols, rwkv_mu[l])
        r, kr, vr, wd, ad, gd = _split_cols(rw_cols, RWKV_COL_SIZES)
        rw = rwkv7_time_mix(r, kr, vr, wd, ad, gd, rwkv_w0[l], rwkv_w2[l], rwkv_a0[l], rwkv_a2[l],
                            rwkv_g2[l], rwkv_k_k[l], rwkv_k_a[l], rwkv_r_k[l], rwkv_ln_w[l], rwkv_ln_b[l])

        h = h + jnp.concatenate([att, rw.astype(h.dtype)], axis=-1) @ w_out[l]

        h = h + moe_ffn(rms_norm(h, norm2_w[l]), router_w[l], router_b[l], exp_w_gu[l], exp_b_gu[l],
                        exp_w_down[l], exp_b_down[l]).astype(h.dtype)
    return h


_drawn_inputs = setup_inputs


def setup_inputs(seed=0):
    import zlib

    import numpy as np

    out = dict(_drawn_inputs(seed))
    spreads = {}
    factors = {'q_norm_w': 3.945,
     'k_norm_w': 3.22,
     'rwkv_ln_b': 3.236,
     'exp_b_gu': 8.0,
     'exp_b_down': 8.0}
    for name, (base, spread) in spreads.items():
        noise = np.random.default_rng([zlib.crc32(name.encode()), seed]).standard_normal(out[name].shape)
        drawn = base * np.exp(spread * noise) if base else spread * noise
        out[name] = jnp.asarray(drawn.astype(out[name].dtype))
    for name, factor in factors.items():
        out[name] = (out[name] * factor).astype(out[name].dtype)
    return out
```

```python
from contextlib import ExitStack

import numpy as np
import concourse.bass as bass
from concourse import mybir

F32 = mybir.dt.float32
BF16 = mybir.dt.bfloat16
I32 = mybir.dt.int32
U32 = mybir.dt.uint32
ALU = mybir.AluOpType
ACT = mybir.ActivationFunctionType
AX = mybir.AxisListType

P = 128
T, D = 512, 1024
NT, KD = T // P, D // P
HD, NH = 64, 8
DH = NH * HD
NP = DH // P
NI, DI = 8, 32
ATT_COLS = 3 * DH + NI * DI + DI + NI
LORA = 128
RW_COLS = 3 * DH + LORA
RW_TILES = RW_COLS // P
N_SEL = min(256, T // 4)
NEG = -3.0e38
OFF = -1.0e30
CH = 64
NC = T // CH
LEVELS = [1, 2, 4, 8, 16, 32]
DECAY = float(np.exp(np.float64(-0.5)))
RMS_EPS, GN_EPS = 1e-6, 64e-5
NE, TOPE, FF = 32, 4, 1024
LIMIT, ALPHA = 7.0, 1.702
MAXB = NE + (T * TOPE) // P
NBT = MAXB + 2
WQ, WK, WV, WI = 0, DH, 2 * DH, 3 * DH

PAR_ROWS = [("norm1_w", KD), ("norm2_w", KD), ("rwkv_mu", RW_TILES), ("rwkv_w0", NP), ("rwkv_a0", NP),
            ("rwkv_k_k", NP), ("rwkv_k_a", NP), ("rwkv_r_k", NP), ("rwkv_ln_w", NP), ("rwkv_ln_b", NP)]
PAR_AT, _n = {}, 0
for _name, _rows in PAR_ROWS:
    PAR_AT[_name] = _n
    _n += _rows
N_PAR = _n


def marks(keys):
    return {k: i + 1 for i, k in enumerate(keys)}


class Chain:

    def __init__(self, engine, sem, start=0):
        self.engine, self.sem, self.n = engine, sem, start

    def __call__(self, ins):
        ins.then_inc(self.sem, 1)
        self.n += 1
        self.engine.wait_ge(self.sem, self.n)


class Places:
    pass


def memory(nc, ctx):
    m = Places()

    def sb(name, cols, dt=F32):
        return ctx.enter_context(nc.sbuf_tensor(name, [P, cols], dt))

    def sem(name):
        return ctx.enter_context(nc.semaphore(name))

    m.sem = sem
    m.h = sb("h", NT * D)
    m.xh = sb("xh", NT * D)
    m.xt = sb("xt", KD * T)
    m.ring = sb("ring", 2 * KD * 512)
    m.w = sb("w", 24 * 1024)
    m.misc = sb("misc", 11 * 512)
    m.con = sb("con", 11 * P)
    m.small = sb("small", 448)
    m.bank = [ctx.enter_context(nc.psum_tensor(f"bank{i}", [P, 512], F32)) for i in range(8)]
    c = [m.con[:, i * P:(i + 1) * P] for i in range(11)]
    m.ident, m.strict, m.incl, m.headsum, m.level = c[0], c[1], c[2], c[3], c[4:10]
    m.parrow = c[10]
    s = m.small
    m.par = s[:, 0:N_PAR]
    m.ommu = s[:, 64:64 + RW_TILES]
    m.ss = s[:, 80:84]
    m.rstd = s[:, 84:88]
    m.pos = s[:, 88:92]
    m.iws = s[:, 96:128]
    m.cos = s[:, 128:160]
    m.sin = s[:, 160:192]
    m.m8 = s[:, 192:200]
    m.nmx = s[:, 200:232]
    m.rsum = s[:, 232:264]
    m.ssq = s[:, 264:328]
    m.ang = s[:, 328:360]
    m.ang2 = s[:, 360:392]
    m.freq = s[:, 392:400]
    m.ssrow = s[:, 400:404]
    m.eps = s[:, 404:408]
    m.dend = s[:, 408:408 + NP * NC]
    m.zr = m.w[:, 17920:17920 + RW_TILES * T].rearrange("p (j t) -> p j t", j=RW_TILES)
    m.xT = m.xt[:, :].rearrange("p (k t) -> p k t", k=KD)
    m.h3 = m.h[:, :].rearrange("p (t d) -> p t d", t=NT)
    m.xh3 = m.xh[:, :].rearrange("p (t d) -> p t d", t=NT)
    m.start = sem("constants_ready")
    return m


def constants(nc, m):
    made = m.sem("mask_made")
    with nc.Block() as block:
        @block.gpsimd
        def _(pool):
            link = Chain(pool, made)
            link(nc.gpsimd.memset(m.con[:, :], 1.0))
            link(nc.gpsimd.affine_select(out=m.ident, in_=m.ident, compare_op=ALU.is_equal, fill=0.0, base=0,
                                         pattern=[[-1, P]], channel_multiplier=1))
            link(nc.gpsimd.affine_select(out=m.strict, in_=m.strict, compare_op=ALU.is_gt, fill=0.0, base=0,
                                         pattern=[[1, P]], channel_multiplier=-1))
            link(nc.gpsimd.affine_select(out=m.incl, in_=m.incl, compare_op=ALU.is_ge, fill=0.0, base=0,
                                         pattern=[[1, P]], channel_multiplier=-1))
            for a in (m.strict, m.incl, m.headsum):
                link(nc.gpsimd.affine_select(out=a[:, CH:P], in_=a[:, CH:P], compare_op=ALU.is_ge, fill=0.0,
                                             base=-CH, pattern=[[0, P - CH]], channel_multiplier=1))
            link(nc.gpsimd.affine_select(out=m.headsum[:, 0:CH], in_=m.headsum[:, 0:CH], compare_op=ALU.is_gt,
                                         fill=0.0, base=CH, pattern=[[0, CH]], channel_multiplier=-1))
            for b, a in zip(LEVELS, m.level):
                nb = P // (2 * b)
                v = a.rearrange("p (n x c) -> p n x c", n=nb, x=2)
                link(nc.gpsimd.memset(v[:, :, 0, :], 0.0))
                w = v[:, :, 1, :]
                link(nc.gpsimd.affine_select(out=w, in_=w, compare_op=ALU.is_ge, fill=0.0, base=0,
                                             pattern=[[-2 * b, nb], [0, b]], channel_multiplier=1))
                link(nc.gpsimd.affine_select(out=w, in_=w, compare_op=ALU.is_gt, fill=0.0, base=b,
                                             pattern=[[2 * b, nb], [0, b]], channel_multiplier=-1))
            for j in range(8):
                link(nc.gpsimd.memset(m.freq[:, j:j + 1], float(np.float32(500000.0) ** np.float32(-j / 8))))
            link(nc.gpsimd.memset(m.eps[:, 0:1], RMS_EPS))
            link(nc.gpsimd.memset(m.eps[:, 1:2], GN_EPS))


def project(nc, m, A):
    ident, bank = m.ident, m.bank
    chunks = [("i", 3 * DH, NI * DI + DI + NI), ("q", WQ, 512), ("k", WK, 512), ("v", WV, 512),
              ("r", ATT_COLS, 512), ("kr", ATT_COLS + DH, 512), ("vr", ATT_COLS + 2 * DH, 512),
              ("lo", ATT_COLS + 3 * DH, LORA)]
    CI = chunks[0][2]
    att = [c[0] for c in chunks[:4]]
    slots = [m.ring[:, 0:4096], m.ring[:, 4096:8192], m.w[:, 0:4096]]

    def chunk_view(n):
        w = chunks[n][2]
        return slots[n % 3][:, 0:KD * w].rearrange("p (k n) -> p k n", k=KD)

    qz = m.xh[:, 0:2048].rearrange("p (t n) -> p t n", t=NT)
    kz = m.xh[:, 2048:4096].rearrange("p (t n) -> p t n", t=NT)
    m.qT = m.w[:, 4096:6144].rearrange("p (c t) -> p c t", c=NP)
    m.kT = m.w[:, 6144:8192].rearrange("p (c t) -> p c t", c=NP)
    m.v = m.w[:, 8192:10240].rearrange("p (t n) -> p t n", t=NT)
    idxT = m.w[:, 10240:11776].rearrange("p (c t) -> p c t", c=3)
    relu = m.w[:, 11776:15872].rearrange("p (h s) -> p h s", h=NI)
    so = [0, 0, 256, 640]
    score = [None] + [m.w[:, 15872 + so[t]:15872 + so[t] + (t + 1) * P] for t in range(1, NT)]
    mo = [0, 128, 384, 768]
    m.maskb = [m.misc[:, mo[t]:mo[t] + (t + 1) * P] for t in range(NT)]
    idxz = m.misc[:, 1280:1280 + NT * CI].rearrange("p (t n) -> p t n", t=NT)
    ikrep = m.misc[:, 2464:2976].rearrange("p (t n) -> p t n", t=NT)
    prev = m.misc[:, 2976:4000].rearrange("p (b t) -> p b t", b=2)
    qkw = m.misc[:, 4000:4128].rearrange("p (a n) -> p a n", a=2)
    rot = m.misc[:, 4128:5152].rearrange("p (a n) -> p a n", a=4)
    sq = m.misc[:, 5152:5632]
    m_sem = m.sem
    x_loaded = [m_sem(f"x_loaded{t}") for t in range(NT)]
    par_loaded, pos_loaded, qkw_loaded = m_sem("par_loaded"), m_sem("pos_loaded"), m_sem("qkw_loaded")
    w_loaded = [m_sem(f"w_in_loaded{i}") for i in range(3)]
    chunk_used, par_up, par_ready = m_sem("chunk_used"), m_sem("par_up"), m_sem("par_ready")
    ss_ready, xhat_ready, x_up = m_sem("squares_summed"), m_sem("xhat_ready"), m_sem("x_transposed")
    rms_var, rms_root = m_sem("rms_var"), m_sem("rms_root")
    xT_act, xT_dve = m_sem("xT_by_act"), m_sem("xT_by_dve")
    proj_up, proj_kept = m_sem("projection_up"), m_sem("projection_kept")
    idx_rot, idxT_up, idxT_kept = m_sem("index_rotated"), m_sem("index_transposed"), m_sem("indexT_kept")
    dot_up, relu_kept, relu_used = m_sem("dots_up"), m_sem("relu_kept"), m_sem("relu_used")
    scored, causal, taken, mask_ok = m_sem("scored"), m_sem("causal"), m_sem("keys_taken"), m_sem("mask_ready")
    ang_ready, trig_ready = m_sem("angles_ready"), m_sem("trig_ready")
    shifted = m_sem("tokens_shifted")
    qk_ss, qk_root, qk_ready, qk_up = m_sem("qk_squares"), m_sem("qk_root"), m_sem("qk_ready"), m_sem("qk_up")
    qkT_act, qkT_dve = m_sem("qkT_by_act"), m_sem("qkT_by_dve")
    dch, ach, pch = m_sem("dve_step"), m_sem("act_step"), m_sem("pool_step")
    groups = [(c, t) for c in range(4) for t in range(NT)]
    groups += [(4 + j // 4, j) for j in range(RW_TILES)]
    DOT_TILES = [3, 2, 1]
    x_dram = A["x"][0].rearrange("(t p) d -> p t d", p=P)
    w_dram = A["w_in"][0].rearrange("(k p) n -> p k n", p=P)

    with nc.Block() as block:
        @block.sync
        def _(sp):
            row = 0
            for t in range(NT):
                sp.dma_start(m.h3[:, t, :], x_dram[:, t, :]).then_inc(x_loaded[t], 16)
            for n in range(len(chunks)):
                if n >= 3:
                    sp.wait_ge(chunk_used, n - 2)
                _, at, w = chunks[n]
                sp.dma_start(chunk_view(n), w_dram[:, :, at:at + w]).then_inc(w_loaded[n % 3], 16)

        @block.gpsimd
        def _(pool):
            for name, rows in PAR_ROWS:
                src = A[name]
                src = src[0].rearrange("a b -> (a b)") if name == "rwkv_r_k" else src[0]
                pool.dma_start(m.parrow[PAR_AT[name]:PAR_AT[name] + rows, :],
                               src.rearrange("(r c) -> r c", c=P)).then_inc(par_loaded, 16)
            pool.dma_start(m.pos.bitcast(I32), A["positions"][0].rearrange("(t p) -> p t", p=P),
                           allow_slow_non_contiguous=True).then_inc(pos_loaded, 16)
            pool.dma_start(qkw[:, 0, :], A["q_norm_w"][0].partition_broadcast(P)).then_inc(qkw_loaded, 16)
            pool.dma_start(qkw[:, 1, :], A["k_norm_w"][0].partition_broadcast(P)).then_inc(qkw_loaded, 16)
            link = Chain(pool, pch)
            link(nc.gpsimd.memset(m.maskb[0], 0.0))
            nc.gpsimd.affine_select(out=m.maskb[0], in_=m.maskb[0], compare_op=ALU.is_ge, fill=OFF, base=0,
                                    pattern=[[-1, P]], channel_multiplier=1).then_inc(mask_ok, 1)

            def causal_scores(n):
                t = DOT_TILES[n]
                pool.wait_ge(scored, n + 1)
                d = score[t][:, t * P:(t + 1) * P]
                nc.gpsimd.affine_select(out=d, in_=d, compare_op=ALU.is_ge, fill=NEG, base=0,
                                        pattern=[[-1, P]], channel_multiplier=1).then_inc(causal, 1)

            def causal_mask(n):
                t = DOT_TILES[n]
                pool.wait_ge(taken, n + 1)
                d = m.maskb[t][:, t * P:(t + 1) * P]
                nc.gpsimd.affine_select(out=d, in_=d, compare_op=ALU.is_ge, fill=OFF, base=0,
                                        pattern=[[-1, P]], channel_multiplier=1).then_inc(mask_ok, 1)

            def shift(j):
                pool.wait_ge(proj_kept, 4 * NT + j + 1)
                nc.gpsimd.tensor_tensor(m.zr[:, j, 1:T], m.zr[:, j, 1:T], prev[:, j % 2, 0:T - 1],
                                        ALU.add).then_inc(shifted, 1)

            causal_scores(0)
            for j in range(0, 2):
                shift(j)
            causal_mask(0)
            causal_scores(1)
            for j in range(2, 6):
                shift(j)
            causal_mask(1)
            causal_scores(2)
            for j in range(6, RW_TILES):
                shift(j)
            causal_mask(2)

        @block.tensor
        def _(pe):
            pe.wait_ge(par_loaded, 16 * len(PAR_ROWS))
            nc.tensor.transpose(bank[0][:, 0:N_PAR], m.parrow[0:N_PAR, :], ident[0:N_PAR, 0:N_PAR]).then_inc(par_up, 1)
            pe.wait_ge(par_ready, 1)
            for t in range(NT):
                pe.wait_ge(xhat_ready, t + 1)
                for k in range(KD):
                    mm = nc.tensor.transpose(bank[k][:, t * P:(t + 1) * P], m.xh3[:, t, k * P:(k + 1) * P], ident)
            mm.then_inc(x_up, 1)

            def group(g):
                n, j = groups[g]
                w = chunk_view(n)
                pe.wait_ge(w_loaded[n % 3], 16 * (n // 3 + 1))
                if g >= 4:
                    pe.wait_ge(proj_kept, g - 3)
                for k in range(KD):
                    if g == 0:
                        pe.wait_ge(xT_dve if k % 2 else xT_act, k // 2 + 1)
                    if n < 4:
                        mm = nc.tensor.matmul(bank[g % 4][:, 0:chunks[n][2]], m.xT[:, k, j * P:(j + 1) * P],
                                              w[:, k, :], start=(k == 0), stop=(k == KD - 1))
                    else:
                        mm = nc.tensor.matmul(bank[g % 4][:, :], w[:, k, (j % 4) * P:(j % 4 + 1) * P],
                                              m.xT[:, k, :], start=(k == 0), stop=(k == KD - 1))
                mm.then_inc(proj_up, 1)
                if g + 1 == len(groups) or groups[g + 1][0] != n:
                    nc.tensor.transpose(bank[7][0:1, 508:509], ident[0:1, 0:1], ident[0:1, 0:1]).then_inc(chunk_used, 1)

            def dots(n):
                t = DOT_TILES[n]
                for h in range(NI):
                    i = NI * n + h
                    if i >= 2:
                        pe.wait_ge(relu_kept, i - 1)
                    o = 32 * (h % 4)
                    nc.tensor.matmul(bank[5 + i % 2][:, 0:(t + 1) * P], idxT[o:o + 32, h // 4, t * P:(t + 1) * P],
                                     idxT[o:o + 32, 2, 0:(t + 1) * P], start=True, stop=True).then_inc(dot_up, 1)

            for g in range(8):
                group(g)
            pe.wait_ge(idx_rot, 1)
            for t in range(NT):
                if t >= 1:
                    pe.wait_ge(idxT_kept, t)
                for c in range(2):
                    nc.tensor.transpose(bank[4][:, c * P:(c + 1) * P], idxz[:, t, c * P:(c + 1) * P], ident)
                nc.tensor.transpose(bank[4][:, 2 * P:3 * P], ikrep[:, t, :], ident).then_inc(idxT_up, 1)
            for g in range(8, 12):
                group(g)
            pe.wait_ge(idxT_kept, NT)
            dots(0)
            for g in range(12, 16):
                group(g)
            dots(1)
            for g in range(16, 20):
                group(g)
            dots(2)
            for g in range(20, len(groups)):
                group(g)
            for i in range(2 * NP):
                pe.wait_ge(qk_ready, 1 if i < NP else 2)
                if i == 0:
                    pe.wait_ge(proj_kept, len(groups))
                src = (qz, kz)[i // NP]
                for t in range(NT):
                    mm = nc.tensor.transpose(bank[i][:, t * P:(t + 1) * P],
                                             src[:, t, (i % NP) * P:(i % NP + 1) * P], ident)
                mm.then_inc(qk_up, 1)

        @block.scalar
        def _(act):
            link = Chain(act, ach)
            for t in range(NT):
                act.wait_ge(x_loaded[t], 16)
                nc.scalar.activation(m.xh3[:, t, :], m.h3[:, t, :], ACT.Square,
                                     accum_out=m.ss[:, t:t + 1]).then_inc(ss_ready, 1)
            act.wait_ge(rms_var, 1)
            nc.scalar.activation(m.rstd, m.ss, ACT.Sqrt).then_inc(rms_root, 1)
            act.wait_ge(ang_ready, 1)
            nc.scalar.activation(m.sin, m.ang, ACT.Sin)
            nc.scalar.activation(m.cos, m.ang2, ACT.Sin).then_inc(trig_ready, 1)
            act.wait_ge(x_up, 1)
            for k in range(0, KD, 2):
                nc.scalar.activation(m.xT[:, k, :], bank[k][:, :], ACT.Copy,
                                     scale=m.par[:, k:k + 1]).then_inc(xT_act, 1)

            def keep(g):
                n, j = groups[g]
                act.wait_ge(proj_up, g + 1)
                if n < 4:
                    if g == 4:
                        act.wait_ge(x_up, 1)
                    dst = (idxz, qz, kz, m.v)[n]
                    nc.scalar.activation(dst[:, j, :], bank[g % 4][:, 0:chunks[n][2]], ACT.Copy).then_inc(proj_kept, 1)
                else:
                    mu = PAR_AT["rwkv_mu"] + j
                    nc.scalar.activation(m.zr[:, j, :], bank[g % 4][:, :], ACT.Copy, scale=m.ommu[:, j:j + 1])
                    if j >= 2:
                        act.wait_ge(shifted, j - 1)
                    nc.scalar.activation(prev[:, j % 2, :], bank[g % 4][:, :], ACT.Copy,
                                         scale=m.par[:, mu:mu + 1]).then_inc(proj_kept, 1)

            def keep_relu(n):
                t = DOT_TILES[n]
                for h in range(NI):
                    i = NI * n + h
                    act.wait_ge(dot_up, i + 1)
                    if n >= 1:
                        act.wait_ge(relu_used, NI * (n - 1) + h + 1)
                    nc.scalar.activation(relu[:, h, 0:(t + 1) * P], bank[5 + i % 2][:, 0:(t + 1) * P],
                                         ACT.Relu).then_inc(relu_kept, 1)

            for g in range(8):
                keep(g)
            for t in range(NT):
                act.wait_ge(idxT_up, t + 1)
                nc.scalar.activation(idxT[:, :, t * P:(t + 1) * P],
                                     bank[4][:, 0:3 * P].rearrange("p (c t) -> p c t", c=3),
                                     ACT.Copy).then_inc(idxT_kept, 1)
            for g in range(8, 12):
                keep(g)
            keep_relu(0)
            for g in range(12, 16):
                keep(g)
            keep_relu(1)
            for g in range(16, 20):
                keep(g)
            keep_relu(2)
            for g in range(20, len(groups)):
                keep(g)
            act.wait_ge(qk_ss, 1)
            nc.scalar.activation(m.ssq, m.ssq, ACT.Sqrt).then_inc(qk_root, 1)
            for i in range(2 * NP):
                act.wait_ge(qk_up, i + 1)
                if i % 2 == 0:
                    dst = (m.qT, m.kT)[i // NP]
                    nc.scalar.activation(dst[:, i % NP, :], bank[i][:, :], ACT.Copy).then_inc(qkT_act, 1)
            act.wait_ge(qkT_act, NP)

        @block.vector
        def _(dve):
            V = nc.vector
            link = Chain(dve, dch)
            dve.wait_ge(par_up, 1)
            V.tensor_copy(m.par, bank[0][:, 0:N_PAR]).then_inc(par_ready, 1)
            dve.wait_ge(par_ready, 1)
            mu0 = PAR_AT["rwkv_mu"]
            link(V.tensor_scalar(m.ommu, m.par[:, mu0:mu0 + RW_TILES], -1.0, 1.0, ALU.mult, ALU.add))
            dve.wait_ge(ss_ready, NT)
            V.tensor_scalar(m.ss, m.ss, 1.0 / D, RMS_EPS, ALU.mult, ALU.add).then_inc(rms_var, 1)
            dve.wait_ge(rms_root, 1)
            link(V.reciprocal(m.rstd, m.rstd))
            for t in range(NT):
                V.tensor_scalar(m.xh3[:, t, :], m.h3[:, t, :], m.rstd[:, t:t + 1], None, ALU.mult).then_inc(xhat_ready, 1)
            dve.wait_ge(pos_loaded, 16)
            link(V.tensor_copy(m.ssrow, m.pos.bitcast(I32)))
            ang3 = m.ang.rearrange("p (t f) -> p t f", t=NT)
            link(V.tensor_tensor(ang3, m.ssrow.unsqueeze(2).to_broadcast([P, NT, 8]),
                                 m.freq.unsqueeze(1).to_broadcast([P, NT, 8]), ALU.mult))
            magic = 12582912.0
            c1 = 6.28125
            c2 = float((np.float32(2 * np.pi - c1).view(np.uint32) & np.uint32(0xFFFFF000)).view(np.float32))
            c3 = float(np.float32(2 * np.pi - c1 - c2))
            link(V.tensor_scalar(m.ang2, m.ang, 1.0 / (2 * np.pi), magic, ALU.mult, ALU.add))
            link(V.tensor_scalar(m.ang2, m.ang2, magic, None, ALU.subtract))
            for c in (c1, c2, c3):
                link(V.scalar_tensor_tensor(out=m.ang, in0=m.ang2, scalar=-c, in1=m.ang, op0=ALU.mult, op1=ALU.add))
            link(V.tensor_scalar(m.ang2, m.ang, float(np.pi / 2), None, ALU.add))
            link(V.tensor_scalar(m.sin, m.ang2, float(np.pi), -2 * float(np.pi), ALU.is_gt, ALU.mult))
            link(V.tensor_tensor(m.ang2, m.ang2, m.sin, ALU.add))
            pi_in = float(np.nextafter(np.float32(np.pi), np.float32(0)))
            V.tensor_scalar(m.ang2, m.ang2, pi_in, -pi_in, ALU.min, ALU.max)
            V.tensor_scalar(m.ang, m.ang, pi_in, -pi_in, ALU.min, ALU.max).then_inc(ang_ready, 1)
            dve.wait_ge(x_up, 1)
            for k in range(1, KD, 2):
                V.tensor_scalar(m.xT[:, k, :], bank[k][:, :], m.par[:, k:k + 1], None, ALU.mult).then_inc(xT_dve, 1)
            cos = m.cos.rearrange("p (t f) -> p t f", t=NT)
            sin = m.sin.rearrange("p (t f) -> p t f", t=NT)

            def rotate(z, heads, half, step, r):
                shape = [P, NT, heads, half]
                c = cos[:, :, 0:8:step].unsqueeze(2).to_broadcast(shape)
                s = sin[:, :, 0:8:step].unsqueeze(2).to_broadcast(shape)
                n = NT * heads * half
                t = [rot[:, i, 0:n].rearrange("p (t h f) -> p t h f", t=NT, h=heads) for i in range(4)]
                x1, x2 = z[:, :, :, 0:half], z[:, :, :, half:2 * half]
                V.tensor_tensor(t[0], x1, c, ALU.mult)
                V.tensor_tensor(t[1], x2, s, ALU.mult)
                V.tensor_tensor(t[2], x2, c, ALU.mult)
                link(V.tensor_tensor(t[3], x1, s, ALU.mult))
                V.tensor_tensor(x1, t[0], t[1], ALU.subtract)
                link(V.tensor_tensor(x2, t[2], t[3], ALU.add))

            dve.wait_ge(trig_ready, 1)
            dve.wait_ge(proj_kept, NT)
            iq = idxz[:, :, 0:NI * DI].rearrange("p t (h d) -> p t h d", h=NI)
            ik = idxz[:, :, NI * DI:(NI + 1) * DI].rearrange("p t (h d) -> p t h d", h=1)
            rotate(iq, NI, 4, 2, rot)
            rotate(ik, 1, 4, 2, rot)
            iws = m.iws.rearrange("p (t h) -> p t h", t=NT)
            V.tensor_scalar(iws, idxz[:, :, (NI + 1) * DI:CI], float((DI * NI) ** -0.5), None, ALU.mult)
            for r in range(4):
                i = V.tensor_copy(ikrep[:, :, r * DI:(r + 1) * DI], idxz[:, :, NI * DI:(NI + 1) * DI])
            i.then_inc(idx_rot, 1)
            dve.wait_ge(idx_rot, 1)
            for n, t in enumerate(DOT_TILES):
                for h in range(NI):
                    dve.wait_ge(relu_kept, NI * n + h + 1)
                    r, w = relu[:, h, 0:(t + 1) * P], iws[:, t, h:h + 1]
                    if h == 0:
                        i = V.tensor_scalar(score[t], r, w, None, ALU.mult)
                    else:
                        i = V.scalar_tensor_tensor(out=score[t], in0=r, scalar=w, in1=score[t], op0=ALU.mult, op1=ALU.add)
                    i.then_inc(relu_used, 1)
                    dve.wait_ge(relu_used, NI * n + h + 1)
                dve.sem_inc(scored, 1)
                dve.wait_ge(causal, n + 1)
                for _ in range(N_SEL // 8):
                    link(V.max(out=m.m8, in_=score[t]))
                    link(V.match_replace(out=score[t], in_to_replace=m.m8, in_values=score[t], imm_value=NEG))
                V.tensor_scalar(m.maskb[t], score[t], NEG, OFF, ALU.is_gt, ALU.mult).then_inc(taken, 1)
            dve.wait_ge(proj_kept, 12)
            dve.wait_ge(qkw_loaded, 32)
            ssq = m.ssq.rearrange("p (a t h) -> p a t h", a=2, t=NT)
            for a, z in enumerate((qz, kz)):
                for t in range(NT):
                    for half in range(2):
                        zz = z[:, t, half * 256:(half + 1) * 256]
                        link(V.tensor_tensor(sq[:, 0:256], zz, zz, ALU.mult))
                        link(V.tensor_reduce(ssq[:, a, t, half * 4:(half + 1) * 4],
                                             sq[:, 0:256].rearrange("p (h d) -> p h d", h=4), AX.X, ALU.add))
            V.tensor_scalar(m.ssq, m.ssq, 1.0 / HD, RMS_EPS, ALU.mult, ALU.add).then_inc(qk_ss, 1)
            link(V.tensor_scalar(qkw[:, 0, :], qkw[:, 0, :], float(HD ** -0.5), None, ALU.mult))
            dve.wait_ge(qk_root, 1)
            link(V.reciprocal(m.ssq, m.ssq))
            for a, z in enumerate((qz, kz)):
                for t in range(NT):
                    zz = z[:, t, :].rearrange("p (h d) -> p h d", h=NH)
                    link(V.tensor_tensor(zz, zz, ssq[:, a, t, :].unsqueeze(2).to_broadcast([P, NH, HD]), ALU.mult))
                    link(V.tensor_tensor(zz, zz, qkw[:, a, :].unsqueeze(1).to_broadcast([P, NH, HD]), ALU.mult))
                rotate(z.rearrange("p t (h d) -> p t h d", h=NH), NH, 8, 1, rot)
                dve.sem_inc(qk_ready, 1)
            for i in range(2 * NP):
                dve.wait_ge(qk_up, i + 1)
                if i % 2 == 1:
                    dst = (m.qT, m.kT)[i // NP]
                    V.tensor_copy(dst[:, i % NP, :], bank[i][:, :]).then_inc(qkT_dve, 1)
            dve.wait_ge(qkT_dve, NP)


def attention(nc, m, A):
    bank, ident = m.bank, m.ident
    qT, kT, v, maskb = m.qT, m.kT, m.v, m.maskb
    units = [(t, h) for t in range(NT) for h in range(NH)]
    NU = len(units)
    logit = m.w[:, 11776:13312].rearrange("p (b s) -> p b s", b=3)
    prob = m.w[:, 13312:14848].rearrange("p (b s) -> p b s", b=3)
    probT = m.w[:, 14848:15872].rearrange("p (b s) -> p b s", b=2)
    SB, TB, OB = bank[0:3], bank[3:5], bank[5:7]
    sem = m.sem
    logits_up, masked, maxed = sem("logits_up"), sem("logits_masked"), sem("row_max_ready")
    exp_done, scaled, prob_up, probT_kept = sem("exp_done"), sem("probs_scaled"), sem("probs_transposed"), sem("probT_kept")
    pv_done, att_kept, dch, rec = sem("pv_done"), sem("att_kept"), sem("att_dve_step"), sem("row_sum_inverted")

    with nc.Block() as block:
        @block.tensor
        def _(pe):
            def scores(u):
                t, h = units[u]
                if u >= 3:
                    pe.wait_ge(masked, u - 2)
                o = HD * (h % 2)
                nc.tensor.matmul(SB[u % 3][:, 0:(t + 1) * P], qT[o:o + HD, h // 2, t * P:(t + 1) * P],
                                 kT[o:o + HD, h // 2, 0:(t + 1) * P], start=True, stop=True).then_inc(logits_up, 1)

            def transposes(u):
                t, h = units[u]
                pe.wait_ge(scaled, u + 1)
                if u >= 2:
                    pe.wait_ge(probT_kept, u - 1)
                for b in range(t + 1):
                    mm = nc.tensor.transpose(TB[u % 2][:, b * P:(b + 1) * P], prob[:, u % 3, b * P:(b + 1) * P], ident)
                mm.then_inc(prob_up, 1)

            def values(u):
                t, h = units[u]
                pe.wait_ge(probT_kept, u + 1)
                if h == 0 and t >= 2:
                    pe.wait_ge(att_kept, t - 1)
                o = HD * (h % 2)
                for b in range(t + 1):
                    mm = nc.tensor.matmul(OB[t % 2][o:o + HD, (h // 2) * P:(h // 2 + 1) * P],
                                          v[:, b, h * HD:(h + 1) * HD], probT[:, u % 2, b * P:(b + 1) * P],
                                          start=(b == 0), stop=(b == t))
                mm.then_inc(pv_done, 1)

            for u in range(NU + 3):
                if u < NU:
                    scores(u)
                if 2 <= u < NU + 2:
                    transposes(u - 2)
                if u >= 3:
                    values(u - 3)

        @block.vector
        def _(dve):
            V = nc.vector
            link = Chain(dve, dch)

            def scale(u):
                t, h = units[u]
                dve.wait_ge(exp_done, u + 1)
                V.reciprocal(m.rsum[:, u:u + 1], m.rsum[:, u:u + 1]).then_inc(rec, 1)
                dve.wait_ge(rec, u + 1)
                p = prob[:, u % 3, 0:(t + 1) * P]
                V.tensor_scalar(p, p, m.rsum[:, u:u + 1], None, ALU.mult).then_inc(scaled, 1)

            for u in range(NU + 1):
                if u < NU:
                    t, h = units[u]
                    dve.wait_ge(logits_up, u + 1)
                    if u >= 3:
                        dve.wait_ge(exp_done, u - 2)
                    lg = logit[:, u % 3, 0:(t + 1) * P]
                    V.tensor_tensor(lg, SB[u % 3][:, 0:(t + 1) * P], maskb[t], ALU.add).then_inc(masked, 1)
                    dve.wait_ge(masked, u + 1)
                    V.tensor_reduce(m.nmx[:, u:u + 1], lg, AX.X, ALU.max, negate=True).then_inc(maxed, 1)
                if u >= 1:
                    scale(u - 1)

        @block.scalar
        def _(act):
            def keep_probT(u):
                t, h = units[u]
                act.wait_ge(prob_up, u + 1)
                if u >= 2:
                    act.wait_ge(pv_done, u - 1)
                nc.scalar.activation(probT[:, u % 2, 0:(t + 1) * P], TB[u % 2][:, 0:(t + 1) * P],
                                     ACT.Copy).then_inc(probT_kept, 1)

            def keep_out(t):
                act.wait_ge(pv_done, NH * (t + 1))
                nc.scalar.activation(m.xT[:, 0:NP, t * P:(t + 1) * P],
                                     OB[t % 2][:, :].rearrange("p (c t) -> p c t", c=NP),
                                     ACT.Copy).then_inc(att_kept, 1)

            for u in range(NU + 4):
                if u < NU:
                    t, h = units[u]
                    act.wait_ge(maxed, u + 1)
                    if u >= 3:
                        act.wait_ge(prob_up, u - 2)
                    nc.scalar.activation(prob[:, u % 3, 0:(t + 1) * P], logit[:, u % 3, 0:(t + 1) * P], ACT.Exp,
                                         bias=m.nmx[:, u:u + 1], accum_out=m.rsum[:, u:u + 1]).then_inc(exp_done, 1)
                if 2 <= u < NU + 2:
                    keep_probT(u - 2)
                if u >= 4 and (u - 4) % NH == NH - 1:
                    keep_out((u - 4) // NH)


def rwkv(nc, m, A):
    bank, ident, xT, zr = m.bank, m.ident, m.xT, m.zr
    par = lambda name, p: m.par[:, PAR_AT[name] + p:PAR_AT[name] + p + 1]

    def area(buf, at, cols, pat, **kw):
        return buf[:, at:at + cols].rearrange(pat, **kw)

    nA = area(m.w, 0, 2048, "p (j t) -> p j t", j=NP)
    nU = area(m.w, 2048, 2048, "p (t n) -> p t n", t=NT)
    KV = area(m.w, 4096, 2048, "p (c j n) -> p c j n", c=NC, j=NP)
    betaE_tok = area(m.w, 6144, 2048, "p (t n) -> p t n", t=NT)
    RB = area(m.w, 8192, 4096, "p (h t) -> p h t", h=NH)
    S = area(m.w, 12288, (NC + 1) * NP * HD, "p (c j n) -> p c j n", c=NC + 1, j=NP)
    nSA = area(m.w, 14592, 2048, "p (t n) -> p t n", t=NT)
    lora_w = m.w[:, 16640:17152]
    L = area(m.xh, 0, 2048, "p (j t) -> p j t", j=NP)
    a = area(m.xh, 2048, 2048, "p (j t) -> p j t", j=NP)
    kk = area(m.ring, 0, 2048, "p (j t) -> p j t", j=NP)
    sq = area(m.ring, 2048, 2048, "p (j t) -> p j t", j=NP)
    n2 = area(m.ring, 4096, 2048, "p (j t) -> p j t", j=NP)
    keepmask = m.ring[:, 6144:6656]
    LT, AK, Tm, TT, Pm, RK = (area(m.ring, 2048 + 1024 * i, 1024, "p (h t) -> p h t", h=2) for i in range(6))
    g = area(m.misc, 0, 2048, "p (j t) -> p j t", j=NP)
    Dd, kapE, betaE, tmp = m.misc[:, 2048:2560], m.misc[:, 2560:3072], m.misc[:, 3072:3584], m.misc[:, 5120:5632]
    al_tok, kapE_tok, v_tok = (area(m.misc, 3584 + 512 * i, 512, "p (t n) -> p t n", t=NT) for i in range(3))
    LTm = [Dd, tmp]
    W1 = area(m.misc, 2560, 512, "p (h t n) -> p h t n", h=2, t=NT)
    omka = m.nmx[:, 0:NP]
    ysq = area(m.xh, 0, 2048, "p (j t) -> p j t", j=NP)
    yrs = area(m.xh, 2048, 2048, "p (j t) -> p j t", j=NP)
    m.wo = m.ring[:, :].rearrange("p (k n) -> p k n", k=KD)
    sem = m.sem
    lora_loaded, lora_act = sem("lora_w_loaded"), sem("lora_inputs_ready")
    up = sem("rwkv_product_up")
    by_act, by_dve = sem("rwkv_taken_by_act"), sem("rwkv_taken_by_dve")
    rate_ok, kprime_ok, sq_ok, n2_max, n2_root, kk_ok = (sem(n) for n in (
        "rates_summed", "k_scaled", "kk_squared", "kk_norm_floored", "kk_norm_root", "kk_normed"))
    decay_ok, inv_ok, rk_ok, vec_ok = sem("decay_ready"), sem("inverse_decay_ready"), sem("rk_ready"), sem("pair_vectors_ready")
    lvl_ok, tt_ok = sem("level_masked"), sem("first_inverse_ready")
    dch, pch, ach = sem("rwkv_dve_step"), sem("rwkv_pool_step"), sem("rwkv_act_step")
    sa_up, sa_ok, ds_up, base_ok, s_ok = (sem(n) for n in (
        "removed_up", "removed_ready", "state_change_up", "state_base_ready", "state_ready"))
    y_up, y_ok, gn_up, gn_ctr, gn_sq, gn_root, mix_ok = (sem(n) for n in (
        "y_up", "y_ready", "gn_product_up", "gn_centred", "gn_squared", "gn_root", "mix_ready"))
    m.wo_loaded = sem("w_out_loaded")

    made = [(("lora", p, x), "act") for p in range(NP) for x in "wag"] + [(("n2", p), "dve") for p in range(NP)]
    for p in range(NP):
        made += [((n, p), "act") for n in ("vT", "alT", "kapT", "betT")] + [(("bonus", p), "dve")]
        made += [((n, p, hh), "dve") for n in ("LT", "AK", "RK", "RB") for hh in range(2)]
        made += [(("T", p, 1, hh), "dve") for hh in range(2)]
        for b in LEVELS[1:]:
            made += [(("P", p, b, hh), "act") for hh in range(2)]
            for hh in range(2):
                made += [(("T", p, b, hh), "dve")] * (b < LEVELS[-1]) + [(("TT", p, b, hh), "dve")]
        made += [(("W1", p), "act"), (("nA", p), "act"), (("U", p), "act"), (("Yv", p), "act")]
        made += [(("KV", p, i), "dve") for i in range(2)]
    n_up = marks([k for k, _ in made])
    taken = {"act": marks([k for k, w in made if w == "act"]), "dve": marks([k for k, w in made if w == "dve"])}
    taker = dict(made)
    taken_sem = {"act": by_act, "dve": by_dve}

    def bk(key):
        return bank[(n_up[key] - 1) % 8]

    def wait_taken(engine, key):
        engine.wait_ge(taken_sem[taker[key]], taken[taker[key]][key])

    def lvl(p, b, hh):
        return (p * len(LEVELS) + LEVELS.index(b)) * 2 + hh + 1

    with nc.Block() as block:
        @block.sync
        def _(sp):
            sp.dma_start(lora_w[0:32, :], A["rwkv_w2"][0]).then_inc(lora_loaded, 16)
            sp.dma_start(lora_w[32:64, :], A["rwkv_a2"][0]).then_inc(lora_loaded, 16)
            sp.dma_start(lora_w[64:128, :], A["rwkv_g2"][0]).then_inc(lora_loaded, 16)
            sp.wait_ge(up, n_up[("KV", NP - 1, 1)])
            sp.wait_ge(by_act, taken["act"][("Yv", NP - 1)])
            sp.dma_start(m.wo, A["w_out"][0].rearrange("(k p) n -> p k n", p=P)).then_inc(m.wo_loaded, 16)

        @block.tensor
        def _(pe):
            def begin(key):
                n = n_up[key]
                if n > 8:
                    wait_taken(pe, made[n - 9][0])
                return bk(key)

            def end(mm):
                mm.then_inc(up, 1)

            MM = nc.tensor.matmul
            pe.wait_ge(lora_loaded, 48)
            pe.wait_ge(lora_act, 1)
            for p in range(NP):
                for x, lo, hi in (("w", 0, 32), ("a", 32, 64), ("g", 64, 128)):
                    o = begin(("lora", p, x))
                    end(MM(o[:, :], lora_w[lo:hi, p * P:(p + 1) * P], zr[lo:hi, 12, :], start=True, stop=True))
            for p in range(NP):
                o = begin(("n2", p))
                pe.wait_ge(sq_ok, p + 1)
                end(MM(o[:, :], m.headsum, sq[:, p, :], start=True, stop=True))
            for p in range(NP):
                pe.wait_ge(vec_ok, p + 1)
                for n, src in (("vT", zr[:, 8 + p, :]), ("alT", kk[:, p, :]), ("kapT", kapE), ("betT", betaE)):
                    o = begin((n, p))
                    for t in range(NT):
                        mm = nc.tensor.transpose(o[:, t * P:(t + 1) * P], src[:, t * P:(t + 1) * P], ident)
                    end(mm)
                o = begin(("bonus", p))
                end(MM(o[:, :], m.headsum, tmp, start=True, stop=True))
                beta, alpha, kappa, rho = a[:, p, :], kk[:, p, :], zr[:, 4 + p, :], zr[:, p, :]
                for n, lhs, rhs in (("LT", beta, alpha), ("AK", kappa, alpha), ("RK", kappa, rho), ("RB", beta, rho)):
                    for hh in range(2):
                        r = slice(HD * hh, HD * (hh + 1))
                        o = begin((n, p, hh))
                        for t in range(NT):
                            c = slice(t * P, (t + 1) * P)
                            mm = MM(o[:, c], lhs[r, c], rhs[r, c], start=True, stop=True)
                        end(mm)

                def tiles(key, lhs, rhs):
                    o = begin(key)
                    for t in range(NT):
                        c = slice(t * P, (t + 1) * P)
                        mm = MM(o[:, c], lhs[:, c], rhs[:, c] if rhs is not None else ident, start=True, stop=True)
                    end(mm)

                for hh in range(2):
                    pe.wait_ge(lvl_ok, lvl(p, 1, hh))
                    tiles(("T", p, 1, hh), LTm[hh], None)
                for b in LEVELS[1:]:
                    for hh in range(2):
                        pe.wait_ge(lvl_ok, lvl(p, b, hh))
                        wait_taken(pe, ("T", p, b // 2, hh))
                        tiles(("P", p, b, hh), LTm[hh], Tm[:, hh, :])
                    for hh in range(2):
                        wait_taken(pe, ("P", p, b, hh))
                        if b == 2:
                            pe.wait_ge(tt_ok, 2 * p + hh + 1)
                        else:
                            wait_taken(pe, ("TT", p, b // 2, hh))
                        if b < LEVELS[-1]:
                            tiles(("T", p, b, hh), TT[:, hh, :], Pm[:, hh, :])
                        tiles(("TT", p, b, hh), Pm[:, hh, :], TT[:, hh, :])
                tc = [slice(t * P, (t + 1) * P) for t in range(NT)]
                hc = [slice(0, HD), slice(HD, P)]
                o = begin(("W1", p))
                wait_taken(pe, ("vT", p))
                for hh in range(2):
                    wait_taken(pe, ("AK", p, hh))
                    for t in range(NT):
                        mm = MM(o[:, hh * 256 + t * HD:hh * 256 + (t + 1) * HD], AK[:, hh, tc[t]],
                                v_tok[:, t, hc[hh]], start=True, stop=True)
                end(mm)
                o = begin(("nA", p))
                wait_taken(pe, ("alT", p))
                for hh in range(2):
                    wait_taken(pe, ("TT", p, LEVELS[-1], hh))
                    for t in range(NT):
                        mm = MM(o[hc[hh], tc[t]], al_tok[:, t, hc[hh]], TT[:, hh, tc[t]], start=True, stop=True)
                end(mm)
                o = begin(("U", p))
                wait_taken(pe, ("W1", p))
                for hh in range(2):
                    for t in range(NT):
                        mm = MM(o[:, t * P + hh * HD:t * P + (hh + 1) * HD], TT[:, hh, tc[t]], W1[:, hh, t, :],
                                start=True, stop=True)
                end(mm)
                o = begin(("Yv", p))
                for hh in range(2):
                    wait_taken(pe, ("RK", p, hh))
                    for t in range(NT):
                        mm = MM(o[hc[hh], tc[t]], v_tok[:, t, hc[hh]], RK[:, hh, tc[t]], start=True, stop=True)
                end(mm)
                wait_taken(pe, ("kapT", p))
                for i in range(2):
                    o = begin(("KV", p, i))
                    for hh in range(2):
                        for t in range(NT):
                            mm = MM(o[hc[hh], t * HD:(t + 1) * HD], kapE_tok[hc[i], t, hc[hh]],
                                    v_tok[hc[i], t, hc[hh]], start=True, stop=True)
                    end(mm)
            pe.wait_ge(by_act, len(taken["act"]))
            pe.wait_ge(by_dve, len(taken["dve"]))
            for c in range(NC):
                r, t = slice(CH * (c % 2), CH * (c % 2 + 1)), c // 2
                pe.wait_ge(s_ok, c + 1)
                for hh in range(2):
                    hr = slice(HD * hh, HD * (hh + 1))
                    for p in range(NP):
                        mm = MM(bank[2 * (c % 2) + hh][r, p * HD:(p + 1) * HD], nA[hr, p, c * CH:(c + 1) * CH],
                                S[hr, c, p, :], start=True, stop=True)
                    mm.then_inc(sa_up, 1)
                pe.wait_ge(sa_ok, 2 * (c + 1))
                for h in range(NH):
                    p, hr = h // 2, slice(HD * (h % 2), HD * (h % 2 + 1))
                    mm = MM(bank[4 + c % 2][hr, p * HD:(p + 1) * HD], betaE_tok[r, t, h * HD:(h + 1) * HD],
                            nSA[r, t, h * HD:(h + 1) * HD], start=True, stop=True)
                mm.then_inc(ds_up, 1)
                if c % 2 == 1:
                    if t >= 2:
                        pe.wait_ge(y_ok, t - 1)
                    for h in range(NH):
                        p, hr = h // 2, slice(HD * (h % 2), HD * (h % 2 + 1))
                        o = bank[6 + t % 2][hr, p * P:(p + 1) * P]
                        MM(o, nSA[:, t, h * HD:(h + 1) * HD], RB[:, h, t * P:(t + 1) * P], start=True, stop=False)
                        for i in range(2):
                            cc = 2 * t + i
                            mm = MM(o[:, i * CH:(i + 1) * CH], S[hr, cc, p, :], zr[hr, p, cc * CH:(cc + 1) * CH],
                                    start=False, stop=(i == 1))
                    mm.then_inc(y_up, 1)
            pe.wait_ge(y_ok, NT)
            for p in range(NP):
                MM(bank[p][:, :], m.headsum, xT[:, NP + p, :], start=True, stop=True).then_inc(gn_up, 1)
            for p in range(NP):
                pe.wait_ge(gn_sq, p + 1)
                MM(bank[4 + p][:, :], m.headsum, ysq[:, p, :], start=True, stop=True).then_inc(gn_up, 1)

        @block.gpsimd
        def _(pool):
            G = nc.gpsimd
            link = Chain(pool, pch)
            for p in range(NP):
                link(G.tensor_scalar(kk[:, p, :], zr[:, 4 + p, :], par("rwkv_k_k", p), None, ALU.mult))
                G.tensor_tensor(sq[:, p, :], kk[:, p, :], kk[:, p, :], ALU.mult).then_inc(sq_ok, 1)
            G.memset(S[:, 0, :, :], 0.0).then_inc(s_ok, 1)
            for p in range(NP):
                for b in LEVELS:
                    mask = m.level[LEVELS.index(b)].unsqueeze(1).to_broadcast([P, NT, P])
                    for hh in range(2):
                        if b == 1:
                            wait_taken(pool, ("LT", p, hh))
                            if hh == 1:
                                pool.wait_ge(up, n_up[("bonus", p)])
                        else:
                            pool.wait_ge(up, n_up[("T", p, 1, hh) if b == 2 else ("P", p, b // 2, hh)])
                            if b == 2:
                                pool.wait_ge(tt_ok, 2 * p + hh + 1)
                        G.tensor_tensor(LTm[hh].rearrange("p (t n) -> p t n", t=NT),
                                        LT[:, hh, :].rearrange("p (t n) -> p t n", t=NT), mask, ALU.mult).then_inc(lvl_ok, 1)
                        if b == 1:
                            pool.wait_ge(lvl_ok, lvl(p, 1, hh))
                            if p >= 1 and hh == 0:
                                pool.wait_ge(up, n_up[("U", p - 1)])
                            G.tensor_tensor(TT[:, hh, :].rearrange("p (t n) -> p t n", t=NT),
                                            ident.unsqueeze(1).to_broadcast([P, NT, P]),
                                            LTm[hh].rearrange("p (t n) -> p t n", t=NT), ALU.subtract).then_inc(tt_ok, 1)
            for c in range(NC - 1):
                pool.wait_ge(s_ok, c + 1)
                if c == 0:
                    pool.wait_ge(by_dve, len(taken["dve"]))
                de = m.dend.rearrange("p (j c) -> p j c", j=NP)[:, :, c:c + 1].to_broadcast([P, NP, HD])
                link(G.tensor_tensor(S[:, c + 1, :, :], S[:, c, :, :], de, ALU.mult))
                G.tensor_tensor(S[:, c + 1, :, :], S[:, c + 1, :, :], KV[:, c, :, :], ALU.add).then_inc(base_ok, 1)

        @block.scalar
        def _(act):
            C = nc.scalar.activation

            def take(key, *args, **kw):
                act.wait_ge(up, n_up[key])
                C(*args, **kw).then_inc(by_act, 1)

            C(zr[0:32, 12, :], zr[0:32, 12, :], ACT.Tanh)
            C(zr[64:128, 12, :], zr[64:128, 12, :], ACT.Sigmoid).then_inc(lora_act, 1)
            for p in range(NP):
                take(("lora", p, "w"), L[:, p, :], bk(("lora", p, "w"))[:, :], ACT.Sigmoid, bias=par("rwkv_w0", p))
                take(("lora", p, "a"), a[:, p, :], bk(("lora", p, "a"))[:, :], ACT.Sigmoid, bias=par("rwkv_a0", p))
                take(("lora", p, "g"), g[:, p, :], bk(("lora", p, "g"))[:, :], ACT.Copy)
            for p in range(NP):
                act.wait_ge(n2_max, p + 1)
                C(n2[:, p, :], n2[:, p, :], ACT.Sqrt).then_inc(n2_root, 1)
            act.wait_ge(rate_ok, NP)
            for p in range(NP):
                if p >= 1:
                    act.wait_ge(up, n_up[("P", p - 1, LEVELS[-1], 1)])
                    act.wait_ge(lvl_ok, lvl(p - 1, LEVELS[-1], 1))
                C(Dd, L[:, p, :], ACT.Exp, scale=-DECAY).then_inc(decay_ok, 1)
                C(L[:, p, :], L[:, p, :], ACT.Exp, scale=DECAY).then_inc(inv_ok, 1)
                if p >= 1:
                    act.wait_ge(up, n_up[("KV", p - 1, 1)])
                for n, dst in (("vT", v_tok[:, :, :]), ("alT", al_tok[:, :, :]), ("kapT", kapE_tok[:, :, :]),
                               ("betT", betaE_tok[:, :, p * P:(p + 1) * P])):
                    take((n, p), dst, bk((n, p))[:, :].rearrange("p (t n) -> p t n", t=NT), ACT.Copy)
                for b in LEVELS[1:]:
                    for hh in range(2):
                        take(("P", p, b, hh), Pm[:, hh, :], bk(("P", p, b, hh))[:, :], ACT.Copy)
                take(("W1", p), W1, bk(("W1", p))[:, :].rearrange("p (h t n) -> p h t n", h=2, t=NT), ACT.Copy)
                take(("nA", p), nA[:, p, :], bk(("nA", p))[:, :], ACT.Copy, scale=-1.0)
                take(("U", p), nU[:, :, p * P:(p + 1) * P], bk(("U", p))[:, :].rearrange("p (t n) -> p t n", t=NT),
                     ACT.Copy, scale=-1.0)
                take(("Yv", p), xT[:, NP + p, :], bk(("Yv", p))[:, :], ACT.Copy)
            for p in range(NP):
                act.wait_ge(gn_ctr, p + 1)
                C(ysq[:, p, :], xT[:, NP + p, :], ACT.Square).then_inc(gn_sq, 1)
            for p in range(NP):
                act.wait_ge(gn_up, NP + p + 1)
                C(yrs[:, p, :], bank[4 + p][:, :], ACT.Sqrt, scale=1.0 / HD, bias=m.eps[:, 1:2]).then_inc(gn_root, 1)

        @block.vector
        def _(dve):
            V = nc.vector
            link = Chain(dve, dch)

            def take(key, ins):
                ins.then_inc(by_dve, 1)

            ka = PAR_AT["rwkv_k_a"]
            link(V.tensor_scalar(omka, m.par[:, ka:ka + NP], -1.0, 1.0, ALU.mult, ALU.add))
            link(V.memset(keepmask, 1.0))
            link(V.memset(keepmask.rearrange("p (c t) -> p c t", c=NC)[:, :, 0:1], 0.0))
            for p in range(NP):
                wait_taken(dve, ("lora", p, "a"))
                V.tensor_tensor_scan(out=L[:, p, :], data0=keepmask, data1=L[:, p, :], initial=0.0, op0=ALU.mult,
                                     op1=ALU.add).then_inc(rate_ok, 1)
                dve.wait_ge(sq_ok, p + 1)
                link(V.tensor_scalar(tmp, a[:, p, :], par("rwkv_k_a", p), omka[:, p:p + 1], ALU.mult, ALU.add))
                link(V.tensor_tensor(zr[:, 4 + p, :], zr[:, 4 + p, :], tmp, ALU.mult))
            for p in range(NP):
                dve.wait_ge(up, n_up[("n2", p)])
                V.tensor_scalar(n2[:, p, :], bk(("n2", p))[:, :], 1e-24, None, ALU.max).then_inc(n2_max, 1)
                dve.sem_inc(by_dve, 1)
            for p in range(NP):
                dve.wait_ge(n2_root, p + 1)
                link(V.reciprocal(n2[:, p, :], n2[:, p, :]))
                link(V.tensor_tensor(kk[:, p, :], kk[:, p, :], n2[:, p, :], ALU.mult))
            c3 = lambda x: x.rearrange("p (c t) -> p c t", c=NC)
            t3 = lambda x: x.rearrange("p (t n) -> p t n", t=NT)
            for p in range(NP):
                r, k, v = zr[:, p, :], zr[:, 4 + p, :], zr[:, 8 + p, :]
                link(V.tensor_tensor(a[:, p, :], a[:, p, :], kk[:, p, :], ALU.mult))
                dve.wait_ge(decay_ok, p + 1)
                link(V.scalar_tensor_tensor(out=tmp, in0=k, scalar=par("rwkv_r_k", p), in1=r, op0=ALU.mult, op1=ALU.mult))
                link(V.tensor_tensor(c3(kk[:, p, :])[:, :, 1:CH], c3(kk[:, p, :])[:, :, 1:CH],
                                     c3(Dd)[:, :, 0:CH - 1], ALU.mult))
                link(V.tensor_tensor(r, r, Dd, ALU.mult))
                dve.wait_ge(inv_ok, p + 1)
                link(V.tensor_tensor(k, k, L[:, p, :], ALU.mult))
                link(V.tensor_tensor(a[:, p, :], a[:, p, :], L[:, p, :], ALU.mult))
                if p >= 1:
                    dve.wait_ge(up, n_up[("U", p - 1)])
                de = c3(Dd)[:, :, CH - 1:CH].to_broadcast([P, NC, CH])
                V.tensor_tensor(c3(kapE), c3(k), de, ALU.mult)
                V.tensor_copy(m.dend.rearrange("p (j c) -> p j c", j=NP)[:, p, :].unsqueeze(2), c3(Dd)[:, :, CH - 1:CH])
                V.tensor_tensor(c3(betaE), c3(a[:, p, :]), de, ALU.mult).then_inc(vec_ok, 1)
                dve.wait_ge(up, n_up[("bonus", p)])
                take(("bonus", p), V.tensor_tensor(v, bk(("bonus", p))[:, :], v, ALU.mult))
                for n, dst, mask in (("LT", LT, m.strict), ("AK", AK, m.strict), ("RK", RK, m.incl), ("RB", None, m.incl)):
                    for hh in range(2):
                        dve.wait_ge(up, n_up[(n, p, hh)])
                        o = RB[:, 2 * p + hh, :] if dst is None else dst[:, hh, :]
                        take((n, p, hh), V.tensor_tensor(t3(o), t3(bk((n, p, hh))[:, :]),
                                                         mask.unsqueeze(1).to_broadcast([P, NT, P]), ALU.mult))
                for hh in range(2):
                    key = ("T", p, 1, hh)
                    dve.wait_ge(up, n_up[key])
                    take(key, V.tensor_tensor(t3(Tm[:, hh, :]), ident.unsqueeze(1).to_broadcast([P, NT, P]),
                                              t3(bk(key)[:, :]), ALU.subtract))
                for b in LEVELS[1:]:
                    for hh in range(2):
                        for n, x in (("T", Tm), ("TT", TT))[b == LEVELS[-1]:]:
                            key = (n, p, b, hh)
                            dve.wait_ge(up, n_up[("TT", p, b, hh)])
                            take(key, V.tensor_tensor(x[:, hh, :], x[:, hh, :], bk(key)[:, :], ALU.subtract))
                for i in range(2):
                    key = ("KV", p, i)
                    dve.wait_ge(up, n_up[key])
                    take(key, V.tensor_copy(KV[:, i:NC:2, p, :],
                                            bk(key)[:, 0:NT * HD].rearrange("p (c n) -> p c n", c=NT)))
            dve.wait_ge(by_act, len(taken["act"]))
            for c in range(NC):
                r, t = slice(CH * (c % 2), CH * (c % 2 + 1)), c // 2
                for hh in range(2):
                    dve.wait_ge(sa_up, 2 * c + hh + 1)
                    odd = lambda x: x[r, t, :].rearrange("p (j n) -> p j n", j=NP)[:, :, hh * HD:(hh + 1) * HD]
                    V.tensor_tensor(odd(nSA), bank[2 * (c % 2) + hh][r, 0:NP * HD].rearrange("p (j n) -> p j n", j=NP),
                                    odd(nU), ALU.add).then_inc(sa_ok, 1)
                dve.wait_ge(ds_up, c + 1)
                if c < NC - 1:
                    dve.wait_ge(base_ok, c + 1)
                    s = S[:, c + 1, :, :]
                    V.tensor_tensor(s, s, bank[4 + c % 2][:, 0:NP * HD].rearrange("p (j n) -> p j n", j=NP),
                                    ALU.add).then_inc(s_ok, 1)
                if c % 2 == 1:
                    dve.wait_ge(y_up, t + 1)
                    y = xT[:, NP:2 * NP, t * P:(t + 1) * P]
                    V.tensor_tensor(y, y, bank[6 + t % 2][:, :].rearrange("p (j n) -> p j n", j=NP),
                                    ALU.add).then_inc(y_ok, 1)
            for p in range(NP):
                y = xT[:, NP + p, :]
                dve.wait_ge(gn_up, p + 1)
                V.scalar_tensor_tensor(out=y, in0=bank[p][:, :], scalar=-1.0 / HD, in1=y, op0=ALU.mult,
                                       op1=ALU.add).then_inc(gn_ctr, 1)
            for p in range(NP):
                y = xT[:, NP + p, :]
                dve.wait_ge(gn_root, p + 1)
                link(V.reciprocal(yrs[:, p, :], yrs[:, p, :]))
                link(V.tensor_tensor(y, y, yrs[:, p, :], ALU.mult))
                link(V.tensor_scalar(y, y, par("rwkv_ln_w", p), par("rwkv_ln_b", p), ALU.mult, ALU.add))
                link(V.tensor_tensor(y, y, zr[:, 8 + p, :], ALU.add))
                link(V.tensor_tensor(y, y, g[:, p, :], ALU.mult))


def route(nc, m, A):
    bank, ident, xT, h3, xh3 = m.bank, m.ident, m.xT, m.h3, m.xh3
    m.bias = m.misc[:, 3072:4608].bitcast(BF16)
    raw = m.misc[:, 0:3072]
    q = m.misc
    m.tabD = q[:, 4608:4808].rearrange("p (t b) -> p t b", t=NT)
    m.tabG = q[:, 4808:5008].rearrange("p (t b) -> p t b", t=NT)
    m.eint = q[:, 5008:5058].bitcast(I32)
    m.nint = q[:, 5058:5059].bitcast(I32)
    m.expert_is = q[:, 5060:5110]
    m.slots = q[:, 5112:5240]
    iotaB, iotaE, pmod = q[:, 5240:5290], q[:, 5290:5322], q[:, 5322:5323]
    rw = q[:, 5324:5580].rearrange("p (k e) -> p k e", k=KD)
    w = m.w[:, 16384:24576]
    before, ones, rb = w[:, 0:128], w[:, 128:256], w[:, 256:288]
    lg = w[:, 512:640].rearrange("p (t e) -> p t e", t=NT)
    top = w[:, 640:672].rearrange("p (t k) -> p t k", t=NT)
    topi = w[:, 672:704].bitcast(U32).rearrange("p (t k) -> p t k", t=NT)
    topf = w[:, 704:736].rearrange("p (t k) -> p t k", t=NT)
    gate = w[:, 736:752].rearrange("p (t k) -> p t k", t=NT)
    gsum, nv0 = w[:, 752:756], w[:, 756:760]
    OH = w[:, 1024:1536].rearrange("p (t k e) -> p t k e", t=NT, k=TOPE)
    prod = w[:, 1536:2048].rearrange("p (t k e) -> p t k e", t=NT, k=TOPE)
    M = w[:, 2048:2176].rearrange("p (t e) -> p t e", t=NT)
    fl = w[:, 2176:2304].rearrange("p (t e) -> p t e", t=NT)
    slot = w[:, 2304:2432].rearrange("p (t e) -> p t e", t=NT)
    blk = w[:, 2432:2560].rearrange("p (t e) -> p t e", t=NT)
    tmp = w[:, 2560:2688].rearrange("p (t e) -> p t e", t=NT)
    nb, bend, bstart = w[:, 2688:2720], w[:, 2720:2752], w[:, 2752:2784]
    blk_k = w[:, 2784:2800].rearrange("p (t k) -> p t k", t=NT)
    slot_k = w[:, 2800:2816].rearrange("p (t k) -> p t k", t=NT)
    eq = w[:, 2816:3016].rearrange("p (t b) -> p t b", t=NT)
    eq2 = w[:, 3016:3216].rearrange("p (t b) -> p t b", t=NT)
    le = w[:, 3216:3216 + NBT * NE].rearrange("p (b e) -> p b e", b=NBT)
    ef = w[:, 4864:4864 + NBT]
    sem = m.sem
    out_up, h_ok, ss_ok, var_ok, root_ok, xh_ok, x_up = (sem(n) for n in (
        "out_up", "h_ready", "h_squared", "h_var", "h_root", "h_normed", "h_transposed"))
    xa, xv, lg_up, rank_up, m_ok = (sem(n) for n in ("hT_by_act", "hT_by_dve", "router_up", "ranks_up", "choice_ready"))
    rb_in, iota_ok, v0_ok, g_ok = sem("router_loaded"), sem("iota_ready"), sem("top_ready"), sem("gates_up")
    bias_in, dch, pch = sem("bias_loaded"), sem("route_dve_step"), sem("route_pool_step")
    m.gu_in = [sem(f"gu_loaded{k}") for k in range(KD)]
    m.dn_in = [sem(f"down_loaded{k}") for k in range(4)]
    m.gu = m.w[:, 0:16384].rearrange("p (k n) -> p k n", k=KD)
    m.gu_dram = A["exp_w_gu"][0].rearrange("e (k p) n -> e p k n", p=P)
    with nc.Block() as block:
        @block.sync
        def _(sp):
            sp.dma_start(rw, A["router_w"][0].rearrange("(k p) e -> p k e", p=P)).then_inc(rb_in, 16)
            sp.dma_start(rb, A["router_b"][0].partition_broadcast(P)).then_inc(rb_in, 16)
            for r in range(3):
                sp.dma_start(raw[NE * r:NE * (r + 1), 0:2 * FF], A["exp_b_gu"][0]).then_inc(bias_in, 16)
                sp.dma_start(raw[NE * r:NE * (r + 1), 2 * FF:3 * FF], A["exp_b_down"][0]).then_inc(bias_in, 16)
            for k in range(KD):
                sp.dma_start(m.gu[:, k, :], m.gu_dram[0, :, k, :]).then_inc(m.gu_in[k], 16)

        @block.gpsimd
        def _(pool):
            G = nc.gpsimd
            link = Chain(pool, pch)
            G.iota(m.slots, [[1, P]], base=0, channel_multiplier=0, allow_small_or_imprecise_dtypes=True)
            G.iota(iotaB, [[1, NBT]], base=-1, channel_multiplier=0, allow_small_or_imprecise_dtypes=True)
            G.iota(iotaE, [[1, NE]], base=0, channel_multiplier=0, allow_small_or_imprecise_dtypes=True)
            link(G.iota(pmod, [[0, 1]], base=0, channel_multiplier=1, allow_small_or_imprecise_dtypes=True))
            link(G.tensor_scalar(pmod[32:64, :], pmod[32:64, :], -32.0, None, ALU.add))
            link(G.tensor_scalar(pmod[64:96, :], pmod[64:96, :], -64.0, None, ALU.add))
            link(G.memset(before, 1.0))
            link(G.memset(ones, 1.0))
            G.affine_select(out=before, in_=before, compare_op=ALU.is_gt, fill=0.0, base=0, pattern=[[1, P]],
                            channel_multiplier=-1).then_inc(iota_ok, 1)
            pool.wait_ge(bias_in, 96)
            link(G.tensor_copy(m.bias[0:96, :], raw[0:96, :]))
            for lo, hi in ((32, 64), (64, 96)):
                link(G.tensor_tensor(raw[lo:hi, :], raw[lo:hi, :], m.bias[lo:hi, :], ALU.subtract))
                link(G.tensor_copy(m.bias[lo:hi, :], raw[lo:hi, :]))
            link(G.tensor_tensor(raw[64:96, :], raw[64:96, :], m.bias[64:96, :], ALU.subtract))
            link(G.tensor_copy(m.bias[64:96, :], raw[64:96, :]))

        @block.tensor
        def _(pe):
            MM = nc.tensor.matmul
            pe.wait_ge(m.wo_loaded, 16)
            for t in range(NT):
                for half in range(2):
                    for k in range(KD):
                        mm = MM(bank[2 * t + half][:, :], xT[:, k, t * P:(t + 1) * P],
                                m.wo[:, k, half * 512:(half + 1) * 512], start=(k == 0), stop=(k == KD - 1))
                    mm.then_inc(out_up, 1)
            pe.wait_ge(h_ok, 2 * NT)
            for t in range(NT):
                pe.wait_ge(xh_ok, t + 1)
                for k in range(KD):
                    mm = nc.tensor.transpose(bank[k][:, t * P:(t + 1) * P], xh3[:, t, k * P:(k + 1) * P], ident)
            mm.then_inc(x_up, 1)
            pe.wait_ge(xa, KD // 2)
            pe.wait_ge(xv, KD // 2)
            pe.wait_ge(rb_in, 32)
            for t in range(NT):
                for k in range(KD):
                    mm = MM(bank[0][:, t * NE:(t + 1) * NE], xT[:, k, t * P:(t + 1) * P], rw[:, k, :],
                            start=(k == 0), stop=(k == KD - 1))
            mm.then_inc(lg_up, 1)
            pe.wait_ge(iota_ok, 1)
            pe.wait_ge(m_ok, 1)
            for t in range(NT):
                for s in range(t + 1):
                    MM(bank[1][:, t * NE:(t + 1) * NE], before if s == t else ones, M[:, s, :], start=(s == 0), stop=(s == t))
            for t in range(NT):
                mm = MM(bank[1][:, NT * NE:(NT + 1) * NE], ones, M[:, t, :], start=(t == 0), stop=(t == NT - 1))
            mm.then_inc(rank_up, 1)

        @block.scalar
        def _(act):
            for t in range(NT):
                act.wait_ge(h_ok, 2 * (t + 1))
                nc.scalar.activation(xh3[:, t, :], h3[:, t, :], ACT.Square, accum_out=m.ss[:, t:t + 1]).then_inc(ss_ok, 1)
            act.wait_ge(var_ok, 1)
            nc.scalar.activation(m.rstd, m.ss, ACT.Sqrt).then_inc(root_ok, 1)
            act.wait_ge(x_up, 1)
            n2 = PAR_AT["norm2_w"]
            for k in range(0, KD, 2):
                nc.scalar.activation(xT[:, k, :], bank[k][:, :], ACT.Copy, scale=m.par[:, n2 + k:n2 + k + 1]).then_inc(xa, 1)
            act.wait_ge(v0_ok, 1)
            for t in range(NT):
                a = nc.scalar.activation(gate[:, t, :], top[:, t, 0:TOPE], ACT.Exp, bias=nv0[:, t:t + 1],
                                         accum_out=gsum[:, t:t + 1])
                a.then_inc(g_ok, 1)

        @block.vector
        def _(dve):
            V = nc.vector
            link = Chain(dve, dch)
            for t in range(NT):
                for half in range(2):
                    dve.wait_ge(out_up, 2 * t + half + 1)
                    hh = h3[:, t, half * 512:(half + 1) * 512]
                    V.tensor_tensor(hh, hh, bank[2 * t + half][:, :], ALU.add).then_inc(h_ok, 1)
            dve.wait_ge(ss_ok, NT)
            V.tensor_scalar(m.ss, m.ss, 1.0 / D, RMS_EPS, ALU.mult, ALU.add).then_inc(var_ok, 1)
            dve.wait_ge(root_ok, 1)
            link(V.reciprocal(m.rstd, m.rstd))
            for t in range(NT):
                V.tensor_scalar(xh3[:, t, :], h3[:, t, :], m.rstd[:, t:t + 1], None, ALU.mult).then_inc(xh_ok, 1)
            dve.wait_ge(x_up, 1)
            n2 = PAR_AT["norm2_w"]
            for k in range(1, KD, 2):
                V.tensor_scalar(xT[:, k, :], bank[k][:, :], m.par[:, n2 + k:n2 + k + 1], None, ALU.mult).then_inc(xv, 1)
            dve.wait_ge(lg_up, 1)
            dve.wait_ge(rb_in, 32)
            link(V.tensor_tensor(lg, bank[0][:, 0:NT * NE].rearrange("p (t e) -> p t e", t=NT),
                                 rb.unsqueeze(1).to_broadcast([P, NT, NE]), ALU.add))
            for t in range(NT):
                link(V.max(out=top[:, t, :], in_=lg[:, t, :]))
                link(V.max_index(out=topi[:, t, :], in_max=top[:, t, :], in_values=lg[:, t, :]))
            V.tensor_scalar(nv0, top[:, :, 0], -1.0, None, ALU.mult).then_inc(v0_ok, 1)
            link(V.tensor_copy(topf, topi))
            dve.wait_ge(iota_ok, 1)
            shape = [P, NT, TOPE, NE]
            link(V.tensor_tensor(OH, iotaE.unsqueeze(1).unsqueeze(1).to_broadcast(shape),
                                 topf[:, :, 0:TOPE].unsqueeze(3).to_broadcast(shape), ALU.is_equal))
            V.tensor_reduce(M, OH.rearrange("p t k e -> p t e k"), AX.X, ALU.add).then_inc(m_ok, 1)
            dve.wait_ge(g_ok, NT)
            link(V.reciprocal(gsum, gsum))
            link(V.tensor_tensor(gate, gate, gsum.unsqueeze(2).to_broadcast([P, NT, TOPE]), ALU.mult))
            dve.wait_ge(rank_up, 1)
            cnt = bank[1][:, NT * NE:(NT + 1) * NE]
            rank = bank[1][:, 0:NT * NE].rearrange("p (t e) -> p t e", t=NT)
            link(V.tensor_scalar(nb, cnt, float(P), 1.0, ALU.is_gt, ALU.add))
            for x in (2, 3):
                link(V.tensor_scalar(bstart, cnt, float(x * P), None, ALU.is_gt))
                link(V.tensor_tensor(nb, nb, bstart, ALU.add))
            link(V.tensor_tensor_scan(out=bend, data0=ones[:, 0:NE], data1=nb, initial=0.0, op0=ALU.mult, op1=ALU.add))
            link(V.tensor_tensor(bstart, bend, nb, ALU.subtract))
            link(V.tensor_scalar(fl, rank, float(P), None, ALU.is_ge))
            for x in (2, 3):
                link(V.tensor_scalar(tmp, rank, float(x * P), None, ALU.is_ge))
                link(V.tensor_tensor(fl, fl, tmp, ALU.add))
            link(V.scalar_tensor_tensor(out=slot, in0=fl, scalar=-float(P), in1=rank, op0=ALU.mult, op1=ALU.add))
            link(V.tensor_scalar(slot, slot, 1.0, None, ALU.add))
            link(V.tensor_tensor(blk, fl, bstart.unsqueeze(1).to_broadcast([P, NT, NE]), ALU.add))
            for src, dst in ((blk, blk_k), (slot, slot_k)):
                link(V.tensor_tensor(prod, OH, src.unsqueeze(2).to_broadcast(shape), ALU.mult))
                link(V.tensor_reduce(dst, prod, AX.X, ALU.add))
            tb = [P, NT, NBT]
            link(V.memset(m.tabD, -1.0))
            link(V.memset(m.tabG, 0.0))
            for k in range(TOPE):
                col = lambda x: x[:, :, k:k + 1].to_broadcast(tb)
                link(V.tensor_tensor(eq, iotaB.unsqueeze(1).to_broadcast(tb), col(blk_k), ALU.is_equal))
                for src, tab in ((slot_k, m.tabD), (gate, m.tabG)):
                    link(V.tensor_tensor(eq2, eq, col(src), ALU.mult))
                    link(V.tensor_tensor(tab, tab, eq2, ALU.add))
            be = [P, NBT, NE]
            link(V.tensor_tensor(le, bend.unsqueeze(1).to_broadcast(be), iotaB.unsqueeze(2).to_broadcast(be), ALU.is_le))
            link(V.tensor_reduce(ef, le, AX.X, ALU.add))
            link(V.tensor_scalar(ef, ef, float(NE - 1), None, ALU.min))
            link(V.tensor_copy(m.eint, ef))
            link(V.tensor_copy(m.nint, bend[:, NE - 1:NE]))
            link(V.tensor_scalar(m.expert_is, ef, pmod, None, ALU.is_equal))


def experts(nc, m, A, out):
    bank, ident, h3, xh3, gu = m.bank, m.ident, m.h3, m.xh3, m.gu
    down = m.w[:, 16384:24576].rearrange("p (k n) -> p k n", k=KD)
    r = m.ring
    xgT = r[:, 0:1024].rearrange("p (k s) -> p k s", k=KD)
    glu, lin, sig = r[:, 1024:2048], r[:, 2048:3072], r[:, 3072:4096]
    actT = r[:, 4096:5120].rearrange("p (k s) -> p k s", k=KD)
    yb = r[:, 5120:6144]
    pick = r[:, 6144:6656].rearrange("p (t s) -> p t s", t=NT)
    place = r[:, 6656:7168].rearrange("p (t s) -> p t s", t=NT)
    who = r[:, 7168:7232].bitcast(BF16)
    gcol, dcol = r[:, 7232:7236], r[:, 7240:7244]
    n2 = PAR_AT["norm2_w"]
    down_dram = A["exp_w_down"][0].rearrange("e (k p) n -> e p k n", p=P)
    out3 = out[0].rearrange("(t p) d -> p t d", p=P)
    sem = m.sem
    gu_used, dn_used = sem("gu_used"), sem("down_used")
    ready = sem("moe_cleared")
    pick_ok, place_up, place_ok, who_ok = sem("pick_ready"), sem("place_up"), sem("place_ready"), sem("who_ready")
    xg_up, xg_ok, h_up, h_taken = sem("gathered_up"), sem("gathered_ready"), sem("hidden_up"), sem("hidden_taken")
    glu_ok, sig_ok, act_ok, actT_up, actT_ok = (sem(n) for n in (
        "glu_ready", "sigmoid_ready", "activation_ready", "actT_up", "actT_ready"))
    y_up, y_ok, add_up, add_ok, stored = (sem(n) for n in (
        "expert_out_up", "expert_out_ready", "scattered_up", "scattered_added", "output_stored"))
    col_ok, step = sem("columns_ready"), sem("moe_dve_step")
    nblocks = dict(min_val=NE, max_val=MAXB - 1)

    with nc.Block() as block:
        @block.sync
        def _(sp):
            for k in range(4):
                sp.dma_start(down[:, 2 * k:2 * k + 2, :], down_dram[0, :, 2 * k:2 * k + 2, :]).then_inc(m.dn_in[k], 16)
            n = sp.value_load(m.nint[0:1, 0:1], **nblocks)
            with sp.Fori(1, n) as b:
                e = sp.value_load(m.eint[0:1, bass.ds(b + 1, 1)], min_val=0, max_val=NE - 1)
                for k in range(KD):
                    sp.wait_ge(gu_used, b * KD + (k + 1 - KD))
                    sp.dma_start(gu[:, k, :], m.gu_dram[bass.ds(e, 1), :, k, :].squeeze(0)).then_inc(m.gu_in[k], 16)
                for k in range(4):
                    sp.wait_ge(dn_used, b * 4 + (k + 1 - 4))
                    sp.dma_start(down[:, 2 * k:2 * k + 2, :],
                                 down_dram[bass.ds(e, 1), :, 2 * k:2 * k + 2, :].squeeze(0)).then_inc(m.dn_in[k], 16)
            for t in range(NT):
                sp.wait_ge(add_ok, n * (2 * NT) + 2 * (t + 1))
                sp.dma_start(out3[:, t, :], h3[:, t, :]).then_inc(stored, 16)
            sp.wait_ge(stored, 16 * NT)

        @block.gpsimd
        def _(pool):
            nc.gpsimd.memset(place, 0.0)
            nc.gpsimd.memset(yb, 0.0).then_inc(ready, 1)

        @block.tensor
        def _(pe):
            MM = nc.tensor.matmul
            n = pe.value_load(m.nint[0:1, 0:1], **nblocks)

            def gather():
                for half in (1, 0):
                    for q in range(4):
                        k = 4 * half + q
                        for t in range(NT):
                            mm = MM(bank[4 + half][:, q * P:(q + 1) * P], xh3[:, t, k * P:(k + 1) * P], pick[:, t, :],
                                    start=(t == 0), stop=(t == NT - 1))
                    mm.then_inc(xg_up, 1)
                    if half == 1:
                        yield

            def scatter(before):
                for i in range(2 * NT):
                    if i >= 2:
                        pe.wait_ge(add_ok, before + (i - 1))
                    MM(bank[6 + i % 2][:, :], place[:, i // 2, :], yb[:, (i % 2) * 512:(i % 2 + 1) * 512],
                       start=True, stop=True).then_inc(add_up, 1)

            pe.wait_ge(pick_ok, 1)
            for _ in gather():
                pass
            pe.wait_ge(ready, 1)
            with pe.Fori(0, n) as b:
                pe.wait_ge(xg_ok, b * 2 + 2)
                for k in range(KD):
                    pe.wait_ge(m.gu_in[k], b * 16 + 16)
                    for j in range(4):
                        mm = MM(bank[j][:, :], xgT[:, k, :], gu[:, k, j * 512:(j + 1) * 512], start=(k == 0), stop=False)
                    mm.then_inc(gu_used, 1)
                    if k == 3:
                        pe.wait_ge(y_ok, b * 2 + 2)
                        for t in range(NT):
                            mm = nc.tensor.transpose(bank[4][:, t * P:(t + 1) * P], pick[:, t, :], ident)
                        mm.then_inc(place_up, 1)
                pe.wait_ge(who_ok, b + 1)
                for j in range(4):
                    mm = MM(bank[j][:, :], who[0:96, :], m.bias[0:96, j * 512:(j + 1) * 512], start=False, stop=True)
                mm.then_inc(h_up, 1)
                scatter(b * (2 * NT))
                pe.wait_ge(pick_ok, b + 2)
                g = gather()
                next(g)
                pe.wait_ge(place_ok, b + 1)
                for _ in g:
                    pass
                pe.wait_ge(act_ok, b + 1)
                for k in range(KD):
                    mm = nc.tensor.transpose(bank[k // 4][:, (k % 4) * P:(k % 4 + 1) * P], glu[:, k * P:(k + 1) * P], ident)
                    if k % 4 == 3:
                        mm.then_inc(actT_up, 1)
                pe.wait_ge(xg_ok, b * 2 + 4)
                for k in range(KD):
                    if k % 4 == 0:
                        pe.wait_ge(actT_ok, b * 2 + (k // 4 + 1))
                    if k % 2 == 0:
                        pe.wait_ge(m.dn_in[k // 2], b * 16 + 16)
                    for j in range(2):
                        mm = MM(bank[4 + j][:, :], actT[:, k, :], down[:, k, j * 512:(j + 1) * 512], start=(k == 0), stop=False)
                    if k % 2 == 1:
                        mm.then_inc(dn_used, 1)
                for j in range(2):
                    mm = MM(bank[4 + j][:, :], who[0:96, :], m.bias[0:96, (4 + j) * 512:(5 + j) * 512], start=False, stop=True)
                mm.then_inc(y_up, 1)
            pe.wait_ge(y_ok, n * 2 + 2)
            scatter(n * (2 * NT))

        @block.scalar
        def _(act):
            C = nc.scalar.activation
            n = act.value_load(m.nint[0:1, 0:1], **nblocks)
            act.wait_ge(ready, 1)
            act.sem_inc(y_ok, 2)
            with act.Fori(0, n) as b:
                act.wait_ge(glu_ok, b + 1)
                C(sig, glu, ACT.Sigmoid, scale=ALPHA).then_inc(sig_ok, 1)
                act.wait_ge(place_up, b + 1)
                act.wait_ge(add_up, b * (2 * NT) + 2 * NT)
                C(place, bank[4][:, :].rearrange("p (t s) -> p t s", t=NT), ACT.Copy).then_inc(place_ok, 1)
                for i in range(2):
                    act.wait_ge(actT_up, b * 2 + (i + 1))
                    C(actT[:, 4 * i:4 * i + 4, :], bank[i][:, :].rearrange("p (k s) -> p k s", k=4),
                      ACT.Copy).then_inc(actT_ok, 1)
                act.wait_ge(y_up, b + 1)
                for j in range(2):
                    C(yb[:, j * 512:(j + 1) * 512], bank[4 + j][:, :], ACT.Copy).then_inc(y_ok, 1)

        @block.vector
        def _(dve):
            V = nc.vector
            n = dve.value_load(m.nint[0:1, 0:1], **nblocks)

            def build_pick():
                shape = [P, NT, P]
                V.tensor_tensor(pick, m.slots.unsqueeze(1).to_broadcast(shape), dcol.unsqueeze(2).to_broadcast(shape),
                                ALU.is_equal).then_inc(pick_ok, 1)

            def keep_gathered(before):
                for i, half in enumerate((1, 0)):
                    dve.wait_ge(xg_up, before + (i + 1))
                    V.tensor_tensor(xgT[:, 4 * half:4 * half + 4, :],
                                    bank[4 + half][:, :].rearrange("p (k s) -> p k s", k=4),
                                    m.par[:, n2 + 4 * half:n2 + 4 * half + 4].unsqueeze(2).to_broadcast([P, 4, P]),
                                    ALU.mult).then_inc(xg_ok, 1)

            def add(i, before):
                dve.wait_ge(add_up, before + (i + 1))
                hh = h3[:, i // 2, (i % 2) * 512:(i % 2 + 1) * 512]
                V.scalar_tensor_tensor(out=hh, in0=bank[6 + i % 2][:, :], scalar=gcol[:, i // 2:i // 2 + 1], in1=hh,
                                       op0=ALU.mult, op1=ALU.add).then_inc(add_ok, 1)

            V.tensor_copy(dcol, m.tabD[:, :, 1]).then_inc(col_ok, 1)
            dve.wait_ge(col_ok, 1)
            build_pick()
            keep_gathered(0)
            with dve.Fori(0, n) as b:
                dve.wait_ge(xg_ok, b * 2 + 2)
                V.tensor_copy(gcol.unsqueeze(2), m.tabG[:, :, bass.ds(b, 1)])
                V.tensor_copy(dcol.unsqueeze(2), m.tabD[:, :, bass.ds(b + 2, 1)]).then_inc(col_ok, 1)
                dve.wait_ge(col_ok, b + 2)
                dve.wait_ge(place_up, b + 1)
                V.tensor_copy(who[0:96, :], m.expert_is[0:96, bass.ds(b + 1, 1)].to_broadcast([96, P])).then_inc(who_ok, 1)
                build_pick()
                before = b * (2 * NT)
                dve.wait_ge(h_up, b + 1)
                for j in range(2):
                    i = V.tensor_scalar(glu[:, j * 512:(j + 1) * 512], bank[j][:, :], LIMIT, None, ALU.min)
                i.then_inc(glu_ok, 1)
                add(0, before)
                add(1, before)
                for j in range(2):
                    i = V.tensor_scalar(lin[:, j * 512:(j + 1) * 512], bank[2 + j][:, :], LIMIT, -LIMIT, ALU.min, ALU.max)
                i.then_inc(step, 1)
                add(2, before)
                add(3, before)
                dve.wait_ge(glu_ok, b + 1)
                dve.wait_ge(step, b + 1)
                V.scalar_tensor_tensor(out=lin, in0=lin, scalar=1.0, in1=glu, op0=ALU.add, op1=ALU.mult).then_inc(h_taken, 1)
                add(4, before)
                add(5, before)
                dve.wait_ge(sig_ok, b + 1)
                dve.wait_ge(h_taken, b + 1)
                V.tensor_tensor(glu, lin, sig, ALU.mult).then_inc(act_ok, 1)
                add(6, before)
                add(7, before)
                keep_gathered(b * 2 + 2)
            dve.wait_ge(xg_ok, n * 2 + 2)
            V.tensor_copy(gcol.unsqueeze(2), m.tabG[:, :, bass.ds(n, 1)]).then_inc(col_ok, 1)
            dve.wait_ge(col_ok, n + 2)
            for i in range(2 * NT):
                add(i, n * (2 * NT))


def build(nc, A, out):
    with ExitStack() as ctx:
        m = memory(nc, ctx)
        constants(nc, m)
        project(nc, m, A)
        attention(nc, m, A)
        rwkv(nc, m, A)
        route(nc, m, A)
        experts(nc, m, A, out)


_INS = ["x", "positions", "norm1_w", "w_in", "q_norm_w", "k_norm_w", "rwkv_mu", "rwkv_w0", "rwkv_w2", "rwkv_a0",
        "rwkv_a2", "rwkv_g2", "rwkv_k_k", "rwkv_k_a", "rwkv_r_k", "rwkv_ln_w", "rwkv_ln_b", "w_out", "norm2_w",
        "router_w", "router_b", "exp_w_gu", "exp_b_gu", "exp_w_down", "exp_b_down"]


def kernel(**inputs):
    import concourse.bacc as _bacc
    from concourse.bass_utils import run_bass_kernel_spmd as _run

    nc = _bacc.Bacc("TRN2", target_bir_lowering=False, num_devices=1)
    arrays, args = {}, {}
    for name in _INS:
        a = np.ascontiguousarray(inputs[name])
        arrays[f"in_{name}"] = a
        args[name] = nc.dram_tensor(f"in_{name}", a.shape, mybir.dt.from_np(a.dtype), kind="ExternalInput").ap()
    out = nc.dram_tensor("out_0", (1, T, D), F32, kind="ExternalOutput").ap()
    build(nc, args, out)
    return _run(nc, [arrays], core_ids=[0]).results[0]["out_0"]
```

```python
from contextlib import ExitStack

import numpy as np
import concourse.bass as bass
from concourse import mybir

F32 = mybir.dt.float32
F32R = mybir.dt.float32r
BF16 = mybir.dt.bfloat16
I32 = mybir.dt.int32
U32 = mybir.dt.uint32
ALU = mybir.AluOpType
ACT = mybir.ActivationFunctionType
AX = mybir.AxisListType

P = 128
T, D = 512, 1024
NT, KD = T // P, D // P
HD, NH = 64, 8
DH = NH * HD
NP = DH // P
NI, DI = 8, 32
ATT_COLS = 3 * DH + NI * DI + DI + NI
LORA = 128
RW_COLS = 3 * DH + LORA
RW_TILES = RW_COLS // P
N_SEL = min(256, T // 4)
NEG = -3.0e38
OFF = -1.0e30
CH = 64
NC = T // CH
LEVELS = [1, 2, 4, 8, 16, 32]
HALF = P // 2
DECAY = float(np.exp(np.float64(-0.5)))
RMS_EPS, GN_EPS = 1e-6, 64e-5
NE, TOPE, FF = 32, 4, 1024
LIMIT, ALPHA = 7.0, 1.702
MAXB = NE + (T * TOPE) // P
NBT = MAXB + 2
WQ, WK, WV, WI = 0, DH, 2 * DH, 3 * DH

PAR_ROWS = [("norm1_w", KD), ("norm2_w", KD), ("rwkv_mu", RW_TILES), ("rwkv_w0", NP), ("rwkv_a0", NP),
            ("rwkv_k_k", NP), ("rwkv_k_a", NP), ("rwkv_r_k", NP), ("rwkv_ln_w", NP), ("rwkv_ln_b", NP)]
PAR_AT, _n = {}, 0
for _name, _rows in PAR_ROWS:
    PAR_AT[_name] = _n
    _n += _rows
N_PAR = _n


def marks(keys):
    return {k: i + 1 for i, k in enumerate(keys)}


class Chain:

    def __init__(self, engine, sem, start=0):
        self.engine, self.sem, self.n = engine, sem, start

    def __call__(self, ins):
        ins.then_inc(self.sem, 1)
        self.n += 1
        self.engine.wait_ge(self.sem, self.n)


class Places:
    pass


def memory(nc, ctx):
    m = Places()
    K = 1024
    base = -(-nc.sbuf_base // 32) * 32
    arena = 46336

    def at(name, offset, cols, dt=F32):
        return nc.alloc_sbuf_tensor_at(name, [P, cols], dt, offset=base + offset)

    def sem(name):
        return ctx.enter_context(nc.semaphore(name))

    m.h = at("h", 0, NT * D)
    m.misc = at("misc", 16 * K, 11 * 512)
    m.con = at("con", 38912, 11 * P)
    m.small = at("small", 44544, 448)
    m.w = at("w", arena, 24 * K)
    m.ring = at("ring", arena + 96 * K, 2 * KD * 512)
    m.xh = at("xh", arena + 128 * K, NT * D)
    m.xt = at("xt", arena + 144 * K, KD * T)
    m.raw = at("weights_raw", arena, 4 * 2048)
    m.xn_hi = at("xn_hi", arena + 32 * K, NT * D, F32R)
    m.xn_lo = at("xn_lo", arena + 48 * K, NT * D, F32R)
    m.w_hi = at("weights_hi", arena + 64 * K, 4 * 2048, F32R)
    m.w_lo = at("weights_lo", arena + 96 * K, 4 * 2048, F32R)
    m.parts = at("parts", arena + 128 * K, 7168, F32R)
    m.sem = sem
    m.bank = [ctx.enter_context(nc.psum_tensor(f"bank{i}", [P, 512], F32)) for i in range(8)]
    c = [m.con[:, i * P:(i + 1) * P] for i in range(11)]
    m.ident, m.strict, m.incl, m.headsum, m.pairs = c[0:5]
    m.level = {b: m.con[:, 5 * P + 64 * i:5 * P + 64 * (i + 1)] for i, b in enumerate(LEVELS[1:])}
    m.parrow = c[10]
    s = m.small
    m.par = s[:, 0:N_PAR]
    m.ommu = s[:, 64:64 + RW_TILES]
    m.ss = s[:, 80:84]
    m.rstd = s[:, 84:88]
    m.pos = s[:, 88:92]
    m.iws = s[:, 96:128]
    m.cos = s[:, 128:160]
    m.sin = s[:, 160:192]
    m.m8 = s[:, 192:200]
    m.nmx = s[:, 200:232]
    m.rsum = s[:, 232:264]
    m.ssq = s[:, 264:328]
    m.ang = s[:, 328:360]
    m.ang2 = s[:, 360:392]
    m.freq = s[:, 392:400]
    m.ssrow = s[:, 400:404]
    m.eps = s[:, 404:408]
    m.heads = m.w[:, 17664:17664 + NP * NH].rearrange("p (j h) -> p j h", j=NP)
    m.spread = m.w[:, 17152:17664]
    m.dend = s[:, 408:408 + NP * NC]
    m.zr = m.w[:, 17920:17920 + RW_TILES * T].rearrange("p (j t) -> p j t", j=RW_TILES)
    m.xT = m.xt[:, :].rearrange("p (k t) -> p k t", k=KD)
    m.h3 = m.h[:, :].rearrange("p (t d) -> p t d", t=NT)
    m.xh3 = m.xh[:, :].rearrange("p (t d) -> p t d", t=NT)
    m.qkw = m.misc[:, 4000:4128].rearrange("p (a n) -> p a n", a=2)
    return m


def constants(nc, m, A):
    made = m.sem("mask_made")
    m.x_loaded = [m.sem(f"x_loaded{t}") for t in range(NT)]
    m.par_loaded, m.pos_loaded, m.qkw_loaded = m.sem("par_loaded"), m.sem("pos_loaded"), m.sem("qkw_loaded")
    x_dram = A["x"][0].rearrange("(t p) d -> p t d", p=P)
    with nc.Block() as block:
        @block.sync
        def _(sp):
            for t in range(NT):
                sp.dma_start(m.h3[:, t, :], x_dram[:, t, :]).then_inc(m.x_loaded[t], 16)

        @block.scalar
        def _(act):
            for name, rows in PAR_ROWS:
                src = A[name]
                src = src[0].rearrange("a b -> (a b)") if name == "rwkv_r_k" else src[0]
                act.dma_start(m.parrow[PAR_AT[name]:PAR_AT[name] + rows, :],
                              src.rearrange("(r c) -> r c", c=P)).then_inc(m.par_loaded, 16)
            act.dma_start(m.pos.bitcast(I32), A["positions"][0].rearrange("(t p) -> p t", p=P),
                          allow_slow_non_contiguous=True).then_inc(m.pos_loaded, 16)
            act.dma_start(m.qkw[:, 0, :], A["q_norm_w"][0].partition_broadcast(P)).then_inc(m.qkw_loaded, 16)
            act.dma_start(m.qkw[:, 1, :], A["k_norm_w"][0].partition_broadcast(P)).then_inc(m.qkw_loaded, 16)

        @block.gpsimd
        def _(pool):
            link = Chain(pool, made)
            link(nc.gpsimd.memset(m.con[:, 0:10 * P], 1.0))
            link(nc.gpsimd.affine_select(out=m.ident, in_=m.ident, compare_op=ALU.is_equal, fill=0.0, base=0,
                                         pattern=[[-1, P]], channel_multiplier=1))
            link(nc.gpsimd.affine_select(out=m.strict, in_=m.strict, compare_op=ALU.is_gt, fill=0.0, base=0,
                                         pattern=[[1, P]], channel_multiplier=-1))
            link(nc.gpsimd.affine_select(out=m.incl, in_=m.incl, compare_op=ALU.is_ge, fill=0.0, base=0,
                                         pattern=[[1, P]], channel_multiplier=-1))
            for a in (m.strict, m.incl, m.headsum):
                link(nc.gpsimd.affine_select(out=a[:, CH:P], in_=a[:, CH:P], compare_op=ALU.is_ge, fill=0.0,
                                             base=-CH, pattern=[[0, P - CH]], channel_multiplier=1))
            link(nc.gpsimd.affine_select(out=m.headsum[:, 0:CH], in_=m.headsum[:, 0:CH], compare_op=ALU.is_gt,
                                         fill=0.0, base=CH, pattern=[[0, CH]], channel_multiplier=-1))
            link(nc.gpsimd.affine_select(out=m.pairs, in_=m.pairs, compare_op=ALU.is_equal, fill=0.0, base=-1,
                                         pattern=[[1, P]], channel_multiplier=-1))
            link(nc.gpsimd.memset(m.pairs.rearrange("p (n x) -> p n x", x=2)[:, :, 0:1], 0.0))
            for b in LEVELS[1:]:
                w = m.level[b].rearrange("p (n c) -> p n c", c=b)
                nb = P // (2 * b)
                link(nc.gpsimd.affine_select(out=w, in_=w, compare_op=ALU.is_ge, fill=0.0, base=-b,
                                             pattern=[[-2 * b, nb], [0, b]], channel_multiplier=1))
                link(nc.gpsimd.affine_select(out=w, in_=w, compare_op=ALU.is_gt, fill=0.0, base=2 * b,
                                             pattern=[[2 * b, nb], [0, b]], channel_multiplier=-1))
            for a, pattern, channel in ((m.heads, [[P, NP], [-HD, NH]], 1), (m.spread, [[1, DH]], -HD)):
                link(nc.gpsimd.memset(a, 1.0))
                link(nc.gpsimd.affine_select(out=a, in_=a, compare_op=ALU.is_ge, fill=0.0, base=0, pattern=pattern,
                                             channel_multiplier=channel))
                link(nc.gpsimd.affine_select(out=a, in_=a, compare_op=ALU.is_gt, fill=0.0, base=HD,
                                             pattern=[[-x, n] for x, n in pattern], channel_multiplier=-channel))
            for j in range(8):
                link(nc.gpsimd.memset(m.freq[:, j:j + 1], float(np.float32(500000.0) ** np.float32(-j / 8))))
            link(nc.gpsimd.memset(m.eps[:, 0:1], RMS_EPS))
            link(nc.gpsimd.memset(m.eps[:, 1:2], GN_EPS))


def project(nc, m, A):
    ident, bank = m.ident, m.bank
    chunks = [("i", 3 * DH, NI * DI + DI + NI), ("q", WQ, 512), ("k", WK, 512), ("v", WV, 512),
              ("r", ATT_COLS, 512), ("kr", ATT_COLS + DH, 512), ("vr", ATT_COLS + 2 * DH, 512),
              ("lo", ATT_COLS + 3 * DH, LORA)]
    CI = chunks[0][2]
    att = [c[0] for c in chunks[:4]]
    slots = [m.ring[:, 0:4096], m.ring[:, 4096:8192], m.w[:, 0:4096]]

    def chunk_view(n):
        w = chunks[n][2]
        return slots[n % 3][:, 0:KD * w].rearrange("p (k n) -> p k n", k=KD)

    qz = m.xh[:, 0:2048].rearrange("p (t n) -> p t n", t=NT)
    kz = m.xh[:, 2048:4096].rearrange("p (t n) -> p t n", t=NT)
    m.qT = m.w[:, 4096:6144].rearrange("p (c t) -> p c t", c=NP)
    m.kT = m.w[:, 6144:8192].rearrange("p (c t) -> p c t", c=NP)
    m.v = m.w[:, 8192:10240].rearrange("p (t n) -> p t n", t=NT)
    idxT = m.w[:, 10240:11776].rearrange("p (c t) -> p c t", c=3)
    relu = m.w[:, 11776:15872].rearrange("p (h s) -> p h s", h=NI)
    so = [0, 0, 256, 640]
    score = [None] + [m.w[:, 15872 + so[t]:15872 + so[t] + (t + 1) * P] for t in range(1, NT)]
    mo = [0, 128, 384, 768]
    m.maskb = [m.misc[:, mo[t]:mo[t] + (t + 1) * P] for t in range(NT)]
    idxz = m.misc[:, 1280:1280 + NT * CI].rearrange("p (t n) -> p t n", t=NT)
    ikrep = m.misc[:, 2464:2976].rearrange("p (t n) -> p t n", t=NT)
    prev = m.misc[:, 2976:4000].rearrange("p (b t) -> p b t", b=2)
    qkw = m.qkw
    rot = m.misc[:, 4128:5152].rearrange("p (a n) -> p a n", a=4)
    sq = m.misc[:, 5152:5632]
    m_sem = m.sem
    x_loaded, par_loaded, pos_loaded, qkw_loaded = m.x_loaded, m.par_loaded, m.pos_loaded, m.qkw_loaded
    w_loaded = [m_sem(f"w_in_loaded{i}") for i in range(3)]
    chunk_used, par_up, par_ready = m_sem("chunk_used"), m_sem("par_up"), m_sem("par_ready")
    ss_ready, xhat_ready, x_up = m_sem("squares_summed"), m_sem("xhat_ready"), m_sem("x_transposed")
    rms_var, rms_root = m_sem("rms_var"), m_sem("rms_root")
    xT_act, xT_dve = m_sem("xT_by_act"), m_sem("xT_by_dve")
    proj_up, proj_kept = m_sem("projection_up"), m_sem("projection_kept")
    idx_rot, idxT_up, idxT_kept = m_sem("index_rotated"), m_sem("index_transposed"), m_sem("indexT_kept")
    dot_up, relu_kept, relu_used = m_sem("dots_up"), m_sem("relu_kept"), m_sem("relu_used")
    scored, causal, taken, mask_ok = m_sem("scored"), m_sem("causal"), m_sem("keys_taken"), m_sem("mask_ready")
    ang_ready, trig_ready = m_sem("angles_ready"), m_sem("trig_ready")
    shifted = m_sem("tokens_shifted")
    qk_ss, qk_root, qk_ready, qk_up = m_sem("qk_squares"), m_sem("qk_root"), m_sem("qk_ready"), m_sem("qk_up")
    qkT_act, qkT_dve = m_sem("qkT_by_act"), m_sem("qkT_by_dve")
    dch, ach, pch = m_sem("dve_step"), m_sem("act_step"), m_sem("pool_step")
    groups = [(c, t) for c in range(4) for t in range(NT)]
    groups += [(4 + j // 4, j) for j in range(RW_TILES)]
    DOT_TILES = [3, 2, 1]
    w_dram = A["w_in"][0].rearrange("(k p) n -> p k n", p=P)

    with nc.Block() as block:
        @block.sync
        def _(sp):
            for n in range(len(chunks)):
                if n >= 3:
                    sp.wait_ge(chunk_used, n - 2)
                _, at, w = chunks[n]
                sp.dma_start(chunk_view(n), w_dram[:, :, at:at + w]).then_inc(w_loaded[n % 3], 16)

        @block.gpsimd
        def _(pool):
            link = Chain(pool, pch)
            link(nc.gpsimd.memset(m.maskb[0], 0.0))
            nc.gpsimd.affine_select(out=m.maskb[0], in_=m.maskb[0], compare_op=ALU.is_ge, fill=OFF, base=0,
                                    pattern=[[-1, P]], channel_multiplier=1).then_inc(mask_ok, 1)

            def causal_scores(n):
                t = DOT_TILES[n]
                pool.wait_ge(scored, n + 1)
                d = score[t][:, t * P:(t + 1) * P]
                nc.gpsimd.affine_select(out=d, in_=d, compare_op=ALU.is_ge, fill=NEG, base=0,
                                        pattern=[[-1, P]], channel_multiplier=1).then_inc(causal, 1)

            def causal_mask(n):
                t = DOT_TILES[n]
                pool.wait_ge(taken, n + 1)
                d = m.maskb[t][:, t * P:(t + 1) * P]
                nc.gpsimd.affine_select(out=d, in_=d, compare_op=ALU.is_ge, fill=OFF, base=0,
                                        pattern=[[-1, P]], channel_multiplier=1).then_inc(mask_ok, 1)

            def shift(j):
                pool.wait_ge(proj_kept, 4 * NT + j + 1)
                nc.gpsimd.tensor_tensor(m.zr[:, j, 1:T], m.zr[:, j, 1:T], prev[:, j % 2, 0:T - 1],
                                        ALU.add).then_inc(shifted, 1)

            causal_scores(0)
            for j in range(0, 2):
                shift(j)
            causal_mask(0)
            causal_scores(1)
            for j in range(2, 6):
                shift(j)
            causal_mask(1)
            causal_scores(2)
            for j in range(6, RW_TILES):
                shift(j)
            causal_mask(2)

        @block.tensor
        def _(pe):
            pe.wait_ge(par_loaded, 16 * len(PAR_ROWS))
            nc.tensor.transpose(bank[0][:, 0:N_PAR], m.parrow[0:N_PAR, :], ident[0:N_PAR, 0:N_PAR]).then_inc(par_up, 1)
            pe.wait_ge(par_ready, 1)
            for t in range(NT):
                pe.wait_ge(xhat_ready, t + 1)
                for k in range(KD):
                    mm = nc.tensor.transpose(bank[k][:, t * P:(t + 1) * P], m.xh3[:, t, k * P:(k + 1) * P], ident)
            mm.then_inc(x_up, 1)

            def group(g):
                n, j = groups[g]
                w = chunk_view(n)
                pe.wait_ge(w_loaded[n % 3], 16 * (n // 3 + 1))
                if g >= 4:
                    pe.wait_ge(proj_kept, g - 3)
                for k in range(KD):
                    if g == 0:
                        pe.wait_ge(xT_dve if k % 2 else xT_act, k // 2 + 1)
                    if n < 4:
                        mm = nc.tensor.matmul(bank[g % 4][:, 0:chunks[n][2]], m.xT[:, k, j * P:(j + 1) * P],
                                              w[:, k, :], start=(k == 0), stop=(k == KD - 1))
                    else:
                        mm = nc.tensor.matmul(bank[g % 4][:, :], w[:, k, (j % 4) * P:(j % 4 + 1) * P],
                                              m.xT[:, k, :], start=(k == 0), stop=(k == KD - 1))
                mm.then_inc(proj_up, 1)
                if g + 1 == len(groups) or groups[g + 1][0] != n:
                    nc.tensor.transpose(bank[7][0:1, 508:509], ident[0:1, 0:1], ident[0:1, 0:1]).then_inc(chunk_used, 1)

            def dots(n):
                t = DOT_TILES[n]
                for h in range(NI):
                    i = NI * n + h
                    if i >= 2:
                        pe.wait_ge(relu_kept, i - 1)
                    o = 32 * (h % 4)
                    nc.tensor.matmul(bank[5 + i % 2][:, 0:(t + 1) * P], idxT[o:o + 32, h // 4, t * P:(t + 1) * P],
                                     idxT[o:o + 32, 2, 0:(t + 1) * P], start=True, stop=True).then_inc(dot_up, 1)

            for g in range(8):
                group(g)
            pe.wait_ge(idx_rot, 1)
            for t in range(NT):
                if t >= 1:
                    pe.wait_ge(idxT_kept, t)
                for c in range(2):
                    nc.tensor.transpose(bank[4][:, c * P:(c + 1) * P], idxz[:, t, c * P:(c + 1) * P], ident)
                nc.tensor.transpose(bank[4][:, 2 * P:3 * P], ikrep[:, t, :], ident).then_inc(idxT_up, 1)
            for g in range(8, 12):
                group(g)
            pe.wait_ge(idxT_kept, NT)
            dots(0)
            for g in range(12, 16):
                group(g)
            dots(1)
            for g in range(16, 20):
                group(g)
            dots(2)
            for g in range(20, len(groups)):
                group(g)
            for i in range(2 * NP):
                pe.wait_ge(qk_ready, 1 if i < NP else 2)
                if i == 0:
                    pe.wait_ge(proj_kept, len(groups))
                src = (qz, kz)[i // NP]
                for t in range(NT):
                    mm = nc.tensor.transpose(bank[i][:, t * P:(t + 1) * P],
                                             src[:, t, (i % NP) * P:(i % NP + 1) * P], ident)
                mm.then_inc(qk_up, 1)

        @block.scalar
        def _(act):
            link = Chain(act, ach)
            for t in range(NT):
                act.wait_ge(x_loaded[t], 16)
                nc.scalar.activation(m.xh3[:, t, :], m.h3[:, t, :], ACT.Square,
                                     accum_out=m.ss[:, t:t + 1]).then_inc(ss_ready, 1)
            act.wait_ge(rms_var, 1)
            nc.scalar.activation(m.rstd, m.ss, ACT.Sqrt).then_inc(rms_root, 1)
            act.wait_ge(ang_ready, 1)
            nc.scalar.activation(m.sin, m.ang, ACT.Sin)
            nc.scalar.activation(m.cos, m.ang2, ACT.Sin).then_inc(trig_ready, 1)
            act.wait_ge(x_up, 1)
            for k in range(0, KD, 2):
                nc.scalar.activation(m.xT[:, k, :], bank[k][:, :], ACT.Copy,
                                     scale=m.par[:, k:k + 1]).then_inc(xT_act, 1)

            def keep(g):
                n, j = groups[g]
                act.wait_ge(proj_up, g + 1)
                if n < 4:
                    if g == 4:
                        act.wait_ge(x_up, 1)
                    dst = (idxz, qz, kz, m.v)[n]
                    nc.scalar.activation(dst[:, j, :], bank[g % 4][:, 0:chunks[n][2]], ACT.Copy).then_inc(proj_kept, 1)
                else:
                    mu = PAR_AT["rwkv_mu"] + j
                    nc.scalar.activation(m.zr[:, j, :], bank[g % 4][:, :], ACT.Copy, scale=m.ommu[:, j:j + 1])
                    if j >= 2:
                        act.wait_ge(shifted, j - 1)
                    nc.scalar.activation(prev[:, j % 2, :], bank[g % 4][:, :], ACT.Copy,
                                         scale=m.par[:, mu:mu + 1]).then_inc(proj_kept, 1)

            def keep_relu(n):
                t = DOT_TILES[n]
                for h in range(NI):
                    i = NI * n + h
                    act.wait_ge(dot_up, i + 1)
                    if n >= 1:
                        act.wait_ge(relu_used, NI * (n - 1) + h + 1)
                    nc.scalar.activation(relu[:, h, 0:(t + 1) * P], bank[5 + i % 2][:, 0:(t + 1) * P],
                                         ACT.Relu).then_inc(relu_kept, 1)

            for g in range(8):
                keep(g)
            for t in range(NT):
                act.wait_ge(idxT_up, t + 1)
                nc.scalar.activation(idxT[:, :, t * P:(t + 1) * P],
                                     bank[4][:, 0:3 * P].rearrange("p (c t) -> p c t", c=3),
                                     ACT.Copy).then_inc(idxT_kept, 1)
            for g in range(8, 12):
                keep(g)
            keep_relu(0)
            for g in range(12, 16):
                keep(g)
            keep_relu(1)
            for g in range(16, 20):
                keep(g)
            keep_relu(2)
            for g in range(20, len(groups)):
                keep(g)
            act.wait_ge(qk_ss, 1)
            nc.scalar.activation(m.ssq, m.ssq, ACT.Sqrt).then_inc(qk_root, 1)
            for i in range(2 * NP):
                act.wait_ge(qk_up, i + 1)
                if i % 2 == 0:
                    dst = (m.qT, m.kT)[i // NP]
                    nc.scalar.activation(dst[:, i % NP, :], bank[i][:, :], ACT.Copy).then_inc(qkT_act, 1)
            act.wait_ge(qkT_act, NP)

        @block.vector
        def _(dve):
            V = nc.vector
            link = Chain(dve, dch)
            dve.wait_ge(par_up, 1)
            V.tensor_copy(m.par, bank[0][:, 0:N_PAR]).then_inc(par_ready, 1)
            dve.wait_ge(par_ready, 1)
            mu0 = PAR_AT["rwkv_mu"]
            link(V.tensor_scalar(m.ommu, m.par[:, mu0:mu0 + RW_TILES], -1.0, 1.0, ALU.mult, ALU.add))
            dve.wait_ge(ss_ready, NT)
            V.tensor_scalar(m.ss, m.ss, 1.0 / D, RMS_EPS, ALU.mult, ALU.add).then_inc(rms_var, 1)
            dve.wait_ge(rms_root, 1)
            link(V.reciprocal(m.rstd, m.rstd))
            for t in range(NT):
                V.tensor_scalar(m.xh3[:, t, :], m.h3[:, t, :], m.rstd[:, t:t + 1], None, ALU.mult).then_inc(xhat_ready, 1)
            dve.wait_ge(pos_loaded, 16)
            link(V.tensor_copy(m.ssrow, m.pos.bitcast(I32)))
            ang3 = m.ang.rearrange("p (t f) -> p t f", t=NT)
            link(V.tensor_tensor(ang3, m.ssrow.unsqueeze(2).to_broadcast([P, NT, 8]),
                                 m.freq.unsqueeze(1).to_broadcast([P, NT, 8]), ALU.mult))
            magic = 12582912.0
            c1 = 6.28125
            c2 = float((np.float32(2 * np.pi - c1).view(np.uint32) & np.uint32(0xFFFFF000)).view(np.float32))
            c3 = float(np.float32(2 * np.pi - c1 - c2))
            link(V.tensor_scalar(m.ang2, m.ang, 1.0 / (2 * np.pi), magic, ALU.mult, ALU.add))
            link(V.tensor_scalar(m.ang2, m.ang2, magic, None, ALU.subtract))
            for c in (c1, c2, c3):
                link(V.scalar_tensor_tensor(out=m.ang, in0=m.ang2, scalar=-c, in1=m.ang, op0=ALU.mult, op1=ALU.add))
            link(V.tensor_scalar(m.ang2, m.ang, float(np.pi / 2), None, ALU.add))
            link(V.tensor_scalar(m.sin, m.ang2, float(np.pi), -2 * float(np.pi), ALU.is_gt, ALU.mult))
            link(V.tensor_tensor(m.ang2, m.ang2, m.sin, ALU.add))
            pi_in = float(np.nextafter(np.float32(np.pi), np.float32(0)))
            V.tensor_scalar(m.ang2, m.ang2, pi_in, -pi_in, ALU.min, ALU.max)
            V.tensor_scalar(m.ang, m.ang, pi_in, -pi_in, ALU.min, ALU.max).then_inc(ang_ready, 1)
            dve.wait_ge(x_up, 1)
            for k in range(1, KD, 2):
                V.tensor_scalar(m.xT[:, k, :], bank[k][:, :], m.par[:, k:k + 1], None, ALU.mult).then_inc(xT_dve, 1)
            cos = m.cos.rearrange("p (t f) -> p t f", t=NT)
            sin = m.sin.rearrange("p (t f) -> p t f", t=NT)

            def rotate(z, heads, half, step, r):
                shape = [P, NT, heads, half]
                c = cos[:, :, 0:8:step].unsqueeze(2).to_broadcast(shape)
                s = sin[:, :, 0:8:step].unsqueeze(2).to_broadcast(shape)
                n = NT * heads * half
                t = [rot[:, i, 0:n].rearrange("p (t h f) -> p t h f", t=NT, h=heads) for i in range(4)]
                x1, x2 = z[:, :, :, 0:half], z[:, :, :, half:2 * half]
                V.tensor_tensor(t[0], x1, c, ALU.mult)
                V.tensor_tensor(t[1], x2, s, ALU.mult)
                V.tensor_tensor(t[2], x2, c, ALU.mult)
                link(V.tensor_tensor(t[3], x1, s, ALU.mult))
                V.tensor_tensor(x1, t[0], t[1], ALU.subtract)
                link(V.tensor_tensor(x2, t[2], t[3], ALU.add))

            dve.wait_ge(trig_ready, 1)
            dve.wait_ge(proj_kept, NT)
            iq = idxz[:, :, 0:NI * DI].rearrange("p t (h d) -> p t h d", h=NI)
            ik = idxz[:, :, NI * DI:(NI + 1) * DI].rearrange("p t (h d) -> p t h d", h=1)
            rotate(iq, NI, 4, 2, rot)
            rotate(ik, 1, 4, 2, rot)
            iws = m.iws.rearrange("p (t h) -> p t h", t=NT)
            V.tensor_scalar(iws, idxz[:, :, (NI + 1) * DI:CI], float((DI * NI) ** -0.5), None, ALU.mult)
            for r in range(4):
                i = V.tensor_copy(ikrep[:, :, r * DI:(r + 1) * DI], idxz[:, :, NI * DI:(NI + 1) * DI])
            i.then_inc(idx_rot, 1)
            dve.wait_ge(idx_rot, 1)
            for n, t in enumerate(DOT_TILES):
                for h in range(NI):
                    dve.wait_ge(relu_kept, NI * n + h + 1)
                    r, w = relu[:, h, 0:(t + 1) * P], iws[:, t, h:h + 1]
                    if h == 0:
                        i = V.tensor_scalar(score[t], r, w, None, ALU.mult)
                    else:
                        i = V.scalar_tensor_tensor(out=score[t], in0=r, scalar=w, in1=score[t], op0=ALU.mult, op1=ALU.add)
                    i.then_inc(relu_used, 1)
                    dve.wait_ge(relu_used, NI * n + h + 1)
                dve.sem_inc(scored, 1)
                dve.wait_ge(causal, n + 1)
                for _ in range(N_SEL // 8):
                    link(V.max(out=m.m8, in_=score[t]))
                    link(V.match_replace(out=score[t], in_to_replace=m.m8, in_values=score[t], imm_value=NEG))
                V.tensor_scalar(m.maskb[t], score[t], NEG, OFF, ALU.is_gt, ALU.mult).then_inc(taken, 1)
            dve.wait_ge(proj_kept, 12)
            dve.wait_ge(qkw_loaded, 32)
            ssq = m.ssq.rearrange("p (a t h) -> p a t h", a=2, t=NT)
            for a, z in enumerate((qz, kz)):
                for t in range(NT):
                    for half in range(2):
                        zz = z[:, t, half * 256:(half + 1) * 256]
                        link(V.tensor_tensor(sq[:, 0:256], zz, zz, ALU.mult))
                        link(V.tensor_reduce(ssq[:, a, t, half * 4:(half + 1) * 4],
                                             sq[:, 0:256].rearrange("p (h d) -> p h d", h=4), AX.X, ALU.add))
            V.tensor_scalar(m.ssq, m.ssq, 1.0 / HD, RMS_EPS, ALU.mult, ALU.add).then_inc(qk_ss, 1)
            link(V.tensor_scalar(qkw[:, 0, :], qkw[:, 0, :], float(HD ** -0.5), None, ALU.mult))
            dve.wait_ge(qk_root, 1)
            link(V.reciprocal(m.ssq, m.ssq))
            for a, z in enumerate((qz, kz)):
                for t in range(NT):
                    zz = z[:, t, :].rearrange("p (h d) -> p h d", h=NH)
                    link(V.tensor_tensor(zz, zz, ssq[:, a, t, :].unsqueeze(2).to_broadcast([P, NH, HD]), ALU.mult))
                    link(V.tensor_tensor(zz, zz, qkw[:, a, :].unsqueeze(1).to_broadcast([P, NH, HD]), ALU.mult))
                rotate(z.rearrange("p t (h d) -> p t h d", h=NH), NH, 8, 1, rot)
                dve.sem_inc(qk_ready, 1)
            for i in range(2 * NP):
                dve.wait_ge(qk_up, i + 1)
                if i % 2 == 1:
                    dst = (m.qT, m.kT)[i // NP]
                    V.tensor_copy(dst[:, i % NP, :], bank[i][:, :]).then_inc(qkT_dve, 1)
            dve.wait_ge(qkT_dve, NP)


def attention(nc, m, A):
    bank, ident = m.bank, m.ident
    qT, kT, v, maskb = m.qT, m.kT, m.v, m.maskb
    units = [(t, h) for t in range(NT) for h in range(NH)]
    NU = len(units)
    logit = m.w[:, 11776:13312].rearrange("p (b s) -> p b s", b=3)
    prob = m.w[:, 13312:14848].rearrange("p (b s) -> p b s", b=3)
    probT = m.w[:, 14848:15872].rearrange("p (b s) -> p b s", b=2)
    SB, TB, OB = bank[0:3], bank[3:5], bank[5:7]
    sem = m.sem
    logits_up, masked, maxed = sem("logits_up"), sem("logits_masked"), sem("row_max_ready")
    exp_done, scaled, prob_up, probT_kept = sem("exp_done"), sem("probs_scaled"), sem("probs_transposed"), sem("probT_kept")
    pv_done, att_kept, dch, rec = sem("pv_done"), sem("att_kept"), sem("att_dve_step"), sem("row_sum_inverted")

    with nc.Block() as block:
        @block.tensor
        def _(pe):
            def scores(u):
                t, h = units[u]
                if u >= 3:
                    pe.wait_ge(masked, u - 2)
                o = HD * (h % 2)
                nc.tensor.matmul(SB[u % 3][:, 0:(t + 1) * P], qT[o:o + HD, h // 2, t * P:(t + 1) * P],
                                 kT[o:o + HD, h // 2, 0:(t + 1) * P], start=True, stop=True).then_inc(logits_up, 1)

            def transposes(u):
                t, h = units[u]
                pe.wait_ge(scaled, u + 1)
                if u >= 2:
                    pe.wait_ge(probT_kept, u - 1)
                for b in range(t + 1):
                    mm = nc.tensor.transpose(TB[u % 2][:, b * P:(b + 1) * P], prob[:, u % 3, b * P:(b + 1) * P], ident)
                mm.then_inc(prob_up, 1)

            def values(u):
                t, h = units[u]
                pe.wait_ge(probT_kept, u + 1)
                if h == 0 and t >= 2:
                    pe.wait_ge(att_kept, t - 1)
                o = HD * (h % 2)
                for b in range(t + 1):
                    mm = nc.tensor.matmul(OB[t % 2][o:o + HD, (h // 2) * P:(h // 2 + 1) * P],
                                          v[:, b, h * HD:(h + 1) * HD], probT[:, u % 2, b * P:(b + 1) * P],
                                          start=(b == 0), stop=(b == t))
                mm.then_inc(pv_done, 1)

            for u in range(NU + 3):
                if u < NU:
                    scores(u)
                if 2 <= u < NU + 2:
                    transposes(u - 2)
                if u >= 3:
                    values(u - 3)

        @block.vector
        def _(dve):
            V = nc.vector
            link = Chain(dve, dch)

            def scale(u):
                t, h = units[u]
                dve.wait_ge(exp_done, u + 1)
                V.reciprocal(m.rsum[:, u:u + 1], m.rsum[:, u:u + 1]).then_inc(rec, 1)
                dve.wait_ge(rec, u + 1)
                p = prob[:, u % 3, 0:(t + 1) * P]
                V.tensor_scalar(p, p, m.rsum[:, u:u + 1], None, ALU.mult).then_inc(scaled, 1)

            for u in range(NU + 1):
                if u < NU:
                    t, h = units[u]
                    dve.wait_ge(logits_up, u + 1)
                    if u >= 3:
                        dve.wait_ge(exp_done, u - 2)
                    lg = logit[:, u % 3, 0:(t + 1) * P]
                    V.tensor_tensor(lg, SB[u % 3][:, 0:(t + 1) * P], maskb[t], ALU.add).then_inc(masked, 1)
                    dve.wait_ge(masked, u + 1)
                    V.tensor_reduce(m.nmx[:, u:u + 1], lg, AX.X, ALU.max, negate=True).then_inc(maxed, 1)
                if u >= 1:
                    scale(u - 1)

        @block.scalar
        def _(act):
            def keep_probT(u):
                t, h = units[u]
                act.wait_ge(prob_up, u + 1)
                if u >= 2:
                    act.wait_ge(pv_done, u - 1)
                nc.scalar.activation(probT[:, u % 2, 0:(t + 1) * P], TB[u % 2][:, 0:(t + 1) * P],
                                     ACT.Copy).then_inc(probT_kept, 1)

            def keep_out(t):
                act.wait_ge(pv_done, NH * (t + 1))
                nc.scalar.activation(m.xT[:, 0:NP, t * P:(t + 1) * P],
                                     OB[t % 2][:, :].rearrange("p (c t) -> p c t", c=NP),
                                     ACT.Copy).then_inc(att_kept, 1)

            for u in range(NU + 4):
                if u < NU:
                    t, h = units[u]
                    act.wait_ge(maxed, u + 1)
                    if u >= 3:
                        act.wait_ge(prob_up, u - 2)
                    nc.scalar.activation(prob[:, u % 3, 0:(t + 1) * P], logit[:, u % 3, 0:(t + 1) * P], ACT.Exp,
                                         bias=m.nmx[:, u:u + 1], accum_out=m.rsum[:, u:u + 1]).then_inc(exp_done, 1)
                if 2 <= u < NU + 2:
                    keep_probT(u - 2)
                if u >= 4 and (u - 4) % NH == NH - 1:
                    keep_out((u - 4) // NH)


def out_bank(m, g):
    return m.bank[(g + 2) % 8]


def out_group(nc, m, g, ks):
    t, half = g // 2, g % 2
    for k in ks:
        mm = nc.tensor.matmul(out_bank(m, g)[:, :], m.xT[:, k, t * P:(t + 1) * P],
                              m.wo[:, k, half * 512:(half + 1) * 512], start=(k == 0), stop=(k == KD - 1))
    return mm


def rwkv(nc, m, A):
    bank, ident, xT, zr = m.bank, m.ident, m.xT, m.zr
    par = lambda name, p: m.par[:, PAR_AT[name] + p:PAR_AT[name] + p + 1]

    def area(buf, at, cols, pat, **kw):
        return buf[:, at:at + cols].rearrange(pat, **kw)

    nA = area(m.w, 0, 2048, "p (j t) -> p j t", j=NP)
    nU = area(m.w, 2048, 2048, "p (t n) -> p t n", t=NT)
    KV = area(m.w, 4096, 2048, "p (c j n) -> p c j n", c=NC, j=NP)
    betaE_tok = area(m.w, 6144, 2048, "p (t n) -> p t n", t=NT)
    RB = area(m.w, 8192, 4096, "p (h t) -> p h t", h=NH)
    S = area(m.w, 12288, (NC + 1) * NP * HD, "p (c j n) -> p c j n", c=NC + 1, j=NP)
    nSA = area(m.w, 14592, 2048, "p (t n) -> p t n", t=NT)
    lora_w = m.w[:, 16640:17152]
    L = area(m.xh, 0, 2048, "p (j t) -> p j t", j=NP)
    a = area(m.xh, 2048, 2048, "p (j t) -> p j t", j=NP)
    kk = area(m.ring, 0, 2048, "p (j t) -> p j t", j=NP)
    sq = area(m.ring, 2048, 2048, "p (j t) -> p j t", j=NP)
    norm = m.w[0:NH, 16640:17152]
    keepmask = m.ring[:, 6144:6656]
    LT, AK, Tm, TT, RK = (area(m.ring, 2048 + 1024 * i, 1024, "p (h t) -> p h t", h=2) for i in (0, 1, 2, 3, 5))
    Pm = area(m.ring, 6144, 512, "p (h t) -> p h t", h=2)
    W1 = area(m.ring, 6656, 512, "p (h t n) -> p h t n", h=2, t=NT)
    g = area(m.misc, 0, 2048, "p (j t) -> p j t", j=NP)
    Dd, kapE, betaE, tmp = m.misc[:, 2048:2560], m.misc[:, 2560:3072], m.misc[:, 3072:3584], m.misc[:, 5120:5632]
    al_tok, kapE_tok, v_tok = (area(m.misc, 3584 + 512 * i, 512, "p (t n) -> p t n", t=NT) for i in range(3))
    LTm = [Dd, tmp]
    omka = m.nmx[:, 0:NP]
    ysq = area(m.xh, 0, 2048, "p (j t) -> p j t", j=NP)
    m.wo = m.ring[:, :].rearrange("p (k n) -> p k n", k=KD)
    sem = m.sem
    lora_loaded, lora_act = sem("lora_w_loaded"), sem("lora_inputs_ready")
    up = sem("rwkv_product_up")
    by_act, by_dve = sem("rwkv_taken_by_act"), sem("rwkv_taken_by_dve")
    rate_ok, sq_ok, n2_max, n2_root, inverted = (sem(n) for n in (
        "rates_summed", "kk_squared", "kk_norm_floored", "kk_norm_root", "norms_inverted"))
    decay_ok, inv_ok, rk_ok, vec_ok = sem("decay_ready"), sem("inverse_decay_ready"), sem("rk_ready"), sem("pair_vectors_ready")
    lvl_ok, tt_ok = sem("level_masked"), sem("first_inverse_ready")
    dch, pch, ach = sem("rwkv_dve_step"), sem("rwkv_pool_step"), sem("rwkv_act_step")
    sa_up, sa_ok, ds_up, base_ok, s_ok = (sem(n) for n in (
        "removed_up", "removed_ready", "state_change_up", "state_base_ready", "state_ready"))
    y_up, y_ok, gn_up, gn_ctr, gn_sq, gn_root, scaled = (sem(n) for n in (
        "y_up", "y_ready", "gn_product_up", "gn_centred", "gn_squared", "gn_root", "mix_scaled"))
    m.wo_loaded = sem("w_out_loaded")

    made = [(("lora", p, x), "act") for p in range(NP) for x in "wag"] + [(("n2",), "dve")]
    made += [(("inv", p), "dve") for p in range(NP)]
    for p in range(NP):
        made += [((n, p), "act") for n in ("vT", "alT", "kapT", "betT")] + [(("bonus", p), "dve")]
        made += [((n, p, hh), "dve") for n in ("LT", "AK", "RK", "RB") for hh in range(2)]
        made += [(("T", p, 1, hh), "dve") for hh in range(2)]
        for b in LEVELS[1:]:
            for hh in range(2):
                made += [(("TT", p, b // 2, hh), "act")] * (b > 2) + [(("P", p, b, hh), "dve")]
            made += [(("T", p, b, hh), "dve") for hh in range(2)]
        made += [(("TT", p, LEVELS[-1], hh), "act") for hh in range(2)]
        made += [(("W1", p), "act"), (("nA", p), "act"), (("U", p), "act"), (("Yv", p), "act")]
        made += [(("KV", p, i), "dve") for i in range(2)]
    n_up = marks([k for k, _ in made])
    taken = {"act": marks([k for k, w in made if w == "act"]), "dve": marks([k for k, w in made if w == "dve"])}
    taker = dict(made)
    taken_sem = {"act": by_act, "dve": by_dve}

    def bk(key):
        return bank[(n_up[key] - 1) % 8]

    def wait_taken(engine, key):
        engine.wait_ge(taken_sem[taker[key]], taken[taker[key]][key])

    def firsts(x, b):
        return x.rearrange("p (t n x c) -> p t n x c", t=NT, x=2, c=b)[:, :, :, 0, :]

    with nc.Block() as block:
        @block.sync
        def _(sp):
            sp.dma_start(lora_w[0:32, :], A["rwkv_w2"][0]).then_inc(lora_loaded, 16)
            sp.dma_start(lora_w[32:64, :], A["rwkv_a2"][0]).then_inc(lora_loaded, 16)
            sp.dma_start(lora_w[64:128, :], A["rwkv_g2"][0]).then_inc(lora_loaded, 16)
            sp.wait_ge(up, n_up[("KV", NP - 1, 1)])
            sp.wait_ge(by_act, taken["act"][("Yv", NP - 1)])
            sp.dma_start(m.wo, A["w_out"][0].rearrange("(k p) n -> p k n", p=P)).then_inc(m.wo_loaded, 16)

        @block.tensor
        def _(pe):
            def begin(key):
                n = n_up[key]
                if n > 8:
                    wait_taken(pe, made[n - 9][0])
                return bk(key)

            def end(mm):
                mm.then_inc(up, 1)

            MM = nc.tensor.matmul
            pe.wait_ge(lora_loaded, 48)
            pe.wait_ge(lora_act, 1)
            for p in range(NP):
                for x, lo, hi in (("w", 0, 32), ("a", 32, 64), ("g", 64, 128)):
                    o = begin(("lora", p, x))
                    end(MM(o[:, :], lora_w[lo:hi, p * P:(p + 1) * P], zr[lo:hi, 12, :], start=True, stop=True))
            o = begin(("n2",))
            for p in range(NP):
                pe.wait_ge(sq_ok, p + 1)
                mm = MM(o[0:NH, :], m.heads[:, p, :], sq[:, p, :], start=(p == 0), stop=(p == NP - 1))
            end(mm)
            pe.wait_ge(inverted, 1)
            for p in range(NP):
                o = begin(("inv", p))
                end(MM(o[:, :], m.spread[0:NH, p * P:(p + 1) * P], norm, start=True, stop=True))
            for p in range(NP):
                pe.wait_ge(vec_ok, p + 1)
                for n, src in (("vT", zr[:, 8 + p, :]), ("alT", kk[:, p, :]), ("kapT", kapE), ("betT", betaE)):
                    o = begin((n, p))
                    for t in range(NT):
                        mm = nc.tensor.transpose(o[:, t * P:(t + 1) * P], src[:, t * P:(t + 1) * P], ident)
                    end(mm)
                o = begin(("bonus", p))
                end(MM(o[:, :], m.headsum, tmp, start=True, stop=True))
                beta, alpha, kappa, rho = a[:, p, :], kk[:, p, :], zr[:, 4 + p, :], zr[:, p, :]
                for n, lhs, rhs in (("LT", beta, alpha), ("AK", kappa, alpha), ("RK", kappa, rho), ("RB", beta, rho)):
                    for hh in range(2):
                        r = slice(HD * hh, HD * (hh + 1))
                        o = begin((n, p, hh))
                        for t in range(NT):
                            c = slice(t * P, (t + 1) * P)
                            mm = MM(o[:, c], lhs[r, c], rhs[r, c], start=True, stop=True)
                        end(mm)

                def turned(key, src):
                    o = begin(key)
                    for t in range(NT):
                        mm = nc.tensor.transpose(o[:, t * P:(t + 1) * P], src[:, t * P:(t + 1) * P], ident)
                    end(mm)

                for hh in range(2):
                    pe.wait_ge(lvl_ok, 2 * p + hh + 1)
                    turned(("T", p, 1, hh), LTm[hh])
                for b in LEVELS[1:]:
                    for hh in range(2):
                        wait_taken(pe, ("T", p, b // 2, hh))
                        if b > 2:
                            turned(("TT", p, b // 2, hh), Tm[:, hh, :])
                        o = begin(("P", p, b, hh))
                        for t in range(NT):
                            mm = MM(o[:, t * HALF:(t + 1) * HALF], LT[:, hh, t * P:(t + 1) * P],
                                    firsts(Tm[:, hh, :], b)[:, t, :, :], start=True, stop=True)
                        end(mm)
                    for hh in range(2):
                        wait_taken(pe, ("P", p, b, hh))
                        if b == 2:
                            pe.wait_ge(tt_ok, 2 * p + hh + 1)
                        else:
                            wait_taken(pe, ("TT", p, b // 2, hh))
                        o = begin(("T", p, b, hh))
                        for t in range(NT):
                            mm = MM(o[:, t * HALF:(t + 1) * HALF], TT[:, hh, t * P:(t + 1) * P],
                                    Pm[:, hh, t * HALF:(t + 1) * HALF], start=True, stop=True)
                        end(mm)
                for hh in range(2):
                    wait_taken(pe, ("T", p, LEVELS[-1], hh))
                    turned(("TT", p, LEVELS[-1], hh), Tm[:, hh, :])
                tc = [slice(t * P, (t + 1) * P) for t in range(NT)]
                hc = [slice(0, HD), slice(HD, P)]
                o = begin(("W1", p))
                wait_taken(pe, ("vT", p))
                for hh in range(2):
                    wait_taken(pe, ("AK", p, hh))
                    for t in range(NT):
                        mm = MM(o[:, hh * 256 + t * HD:hh * 256 + (t + 1) * HD], AK[:, hh, tc[t]],
                                v_tok[:, t, hc[hh]], start=True, stop=True)
                end(mm)
                o = begin(("nA", p))
                wait_taken(pe, ("alT", p))
                for hh in range(2):
                    wait_taken(pe, ("TT", p, LEVELS[-1], hh))
                    for t in range(NT):
                        mm = MM(o[hc[hh], tc[t]], al_tok[:, t, hc[hh]], TT[:, hh, tc[t]], start=True, stop=True)
                end(mm)
                o = begin(("U", p))
                wait_taken(pe, ("W1", p))
                for hh in range(2):
                    for t in range(NT):
                        mm = MM(o[:, t * P + hh * HD:t * P + (hh + 1) * HD], TT[:, hh, tc[t]], W1[:, hh, t, :],
                                start=True, stop=True)
                end(mm)
                o = begin(("Yv", p))
                for hh in range(2):
                    wait_taken(pe, ("RK", p, hh))
                    for t in range(NT):
                        mm = MM(o[hc[hh], tc[t]], v_tok[:, t, hc[hh]], RK[:, hh, tc[t]], start=True, stop=True)
                end(mm)
                wait_taken(pe, ("kapT", p))
                for i in range(2):
                    o = begin(("KV", p, i))
                    for hh in range(2):
                        for t in range(NT):
                            mm = MM(o[hc[hh], t * HD:(t + 1) * HD], kapE_tok[hc[i], t, hc[hh]],
                                    v_tok[hc[i], t, hc[hh]], start=True, stop=True)
                    end(mm)
            pe.wait_ge(by_act, len(taken["act"]))
            pe.wait_ge(by_dve, len(taken["dve"]))
            for c in range(NC):
                r, t = slice(CH * (c % 2), CH * (c % 2 + 1)), c // 2
                pe.wait_ge(s_ok, c + 1)
                for hh in range(2):
                    hr = slice(HD * hh, HD * (hh + 1))
                    for p in range(NP):
                        mm = MM(bank[2 * (c % 2) + hh][r, p * HD:(p + 1) * HD], nA[hr, p, c * CH:(c + 1) * CH],
                                S[hr, c, p, :], start=True, stop=True)
                    mm.then_inc(sa_up, 1)
                pe.wait_ge(sa_ok, 2 * (c + 1))
                for h in range(NH):
                    p, hr = h // 2, slice(HD * (h % 2), HD * (h % 2 + 1))
                    mm = MM(bank[4 + c % 2][hr, p * HD:(p + 1) * HD], betaE_tok[r, t, h * HD:(h + 1) * HD],
                            nSA[r, t, h * HD:(h + 1) * HD], start=True, stop=True)
                mm.then_inc(ds_up, 1)
                if c % 2 == 1:
                    if t >= 2:
                        pe.wait_ge(y_ok, t - 1)
                    for h in range(NH):
                        p, hr = h // 2, slice(HD * (h % 2), HD * (h % 2 + 1))
                        o = bank[6 + t % 2][hr, p * P:(p + 1) * P]
                        MM(o, nSA[:, t, h * HD:(h + 1) * HD], RB[:, h, t * P:(t + 1) * P], start=True, stop=False)
                        for i in range(2):
                            cc = 2 * t + i
                            mm = MM(o[:, i * CH:(i + 1) * CH], S[hr, cc, p, :], zr[hr, p, cc * CH:(cc + 1) * CH],
                                    start=False, stop=(i == 1))
                    mm.then_inc(y_up, 1)
            pe.wait_ge(y_ok, NT)
            pe.wait_ge(m.wo_loaded, 16)

            def head_sum(p):
                if p >= 2:
                    pe.wait_ge(gn_ctr, p - 1)
                MM(bank[p % 2][:, :], m.headsum, xT[:, NP + p, :], start=True, stop=True).then_inc(gn_up, 1)

            def spread_root(p):
                if p >= 2:
                    pe.wait_ge(scaled, p - 1)
                MM(bank[p % 2][:, :], m.spread[0:NH, p * P:(p + 1) * P], norm, start=True, stop=True).then_inc(gn_up, 1)

            head_sum(0)
            head_sum(1)
            out_group(nc, m, 0, range(NP))
            head_sum(2)
            head_sum(3)
            out_group(nc, m, 1, range(NP))
            pe.wait_ge(gn_ctr, NP)
            for p in range(NP):
                pe.wait_ge(gn_sq, p + 1)
                mm = MM(bank[0][0:NH, :], m.heads[:, p, :], ysq[:, p, :], start=(p == 0), stop=(p == NP - 1))
            mm.then_inc(gn_up, 1)
            out_group(nc, m, 2, range(NP))
            out_group(nc, m, 3, range(NP))
            pe.wait_ge(inverted, 2)
            spread_root(0)
            spread_root(1)
            out_group(nc, m, 4, range(NP))
            spread_root(2)
            spread_root(3)
            out_group(nc, m, 5, range(NP))

        @block.gpsimd
        def _(pool):
            G = nc.gpsimd
            link = Chain(pool, pch)
            for p in range(NP):
                link(G.tensor_scalar(kk[:, p, :], zr[:, 4 + p, :], par("rwkv_k_k", p), None, ALU.mult))
                G.tensor_tensor(sq[:, p, :], kk[:, p, :], kk[:, p, :], ALU.mult).then_inc(sq_ok, 1)
            G.memset(S[:, 0, :, :], 0.0).then_inc(s_ok, 1)
            for p in range(NP):
                for hh in range(2):
                    wait_taken(pool, ("LT", p, hh))
                    if hh == 1:
                        pool.wait_ge(up, n_up[("bonus", p)])
                    G.tensor_tensor(LTm[hh].rearrange("p (t n) -> p t n", t=NT),
                                    LT[:, hh, :].rearrange("p (t n) -> p t n", t=NT),
                                    m.pairs.unsqueeze(1).to_broadcast([P, NT, P]), ALU.mult).then_inc(lvl_ok, 1)
                    pool.wait_ge(lvl_ok, 2 * p + hh + 1)
                    if p >= 1 and hh == 0:
                        pool.wait_ge(up, n_up[("U", p - 1)])
                    G.tensor_tensor(TT[:, hh, :].rearrange("p (t n) -> p t n", t=NT),
                                    ident.unsqueeze(1).to_broadcast([P, NT, P]),
                                    LTm[hh].rearrange("p (t n) -> p t n", t=NT), ALU.subtract).then_inc(tt_ok, 1)
            for c in range(NC - 1):
                pool.wait_ge(s_ok, c + 1)
                if c == 0:
                    pool.wait_ge(by_dve, len(taken["dve"]))
                de = m.dend.rearrange("p (j c) -> p j c", j=NP)[:, :, c:c + 1].to_broadcast([P, NP, HD])
                link(G.tensor_tensor(S[:, c + 1, :, :], S[:, c, :, :], de, ALU.mult))
                G.tensor_tensor(S[:, c + 1, :, :], S[:, c + 1, :, :], KV[:, c, :, :], ALU.add).then_inc(base_ok, 1)

        @block.scalar
        def _(act):
            C = nc.scalar.activation

            def take(key, *args, **kw):
                act.wait_ge(up, n_up[key])
                C(*args, **kw).then_inc(by_act, 1)

            C(zr[0:32, 12, :], zr[0:32, 12, :], ACT.Tanh)
            C(zr[64:128, 12, :], zr[64:128, 12, :], ACT.Sigmoid).then_inc(lora_act, 1)
            for p in range(NP):
                take(("lora", p, "w"), L[:, p, :], bk(("lora", p, "w"))[:, :], ACT.Sigmoid, bias=par("rwkv_w0", p))
                take(("lora", p, "a"), a[:, p, :], bk(("lora", p, "a"))[:, :], ACT.Sigmoid, bias=par("rwkv_a0", p))
                take(("lora", p, "g"), g[:, p, :], bk(("lora", p, "g"))[:, :], ACT.Copy)
            def decays(p):
                C(Dd, L[:, p, :], ACT.Exp, scale=-DECAY).then_inc(decay_ok, 1)
                C(L[:, p, :], L[:, p, :], ACT.Exp, scale=DECAY).then_inc(inv_ok, 1)

            act.wait_ge(n2_max, 1)
            C(norm, norm, ACT.Sqrt).then_inc(n2_root, 1)
            act.wait_ge(rate_ok, NP)
            decays(0)
            for p in range(NP):
                if p >= 1:
                    act.wait_ge(up, n_up[("KV", p - 1, 1)])
                for n, dst in (("vT", v_tok[:, :, :]), ("alT", al_tok[:, :, :]), ("kapT", kapE_tok[:, :, :]),
                               ("betT", betaE_tok[:, :, p * P:(p + 1) * P])):
                    take((n, p), dst, bk((n, p))[:, :].rearrange("p (t n) -> p t n", t=NT), ACT.Copy)
                if p < NP - 1:
                    act.wait_ge(up, n_up[("T", p, 1, 1)])
                    act.wait_ge(tt_ok, 2 * p + 2)
                    decays(p + 1)
                for b in LEVELS[1:]:
                    for hh in range(2):
                        take(("TT", p, b, hh), TT[:, hh, :], bk(("TT", p, b, hh))[:, :], ACT.Copy)
                take(("W1", p), W1, bk(("W1", p))[:, :].rearrange("p (h t n) -> p h t n", h=2, t=NT), ACT.Copy)
                take(("nA", p), nA[:, p, :], bk(("nA", p))[:, :], ACT.Copy, scale=-1.0)
                take(("U", p), nU[:, :, p * P:(p + 1) * P], bk(("U", p))[:, :].rearrange("p (t n) -> p t n", t=NT),
                     ACT.Copy, scale=-1.0)
                take(("Yv", p), xT[:, NP + p, :], bk(("Yv", p))[:, :], ACT.Copy)
            for p in range(NP):
                act.wait_ge(gn_ctr, p + 1)
                C(ysq[:, p, :], xT[:, NP + p, :], ACT.Square).then_inc(gn_sq, 1)
            act.wait_ge(gn_up, NP + 1)
            C(norm, bank[0][0:NH, :], ACT.Sqrt, scale=1.0 / HD, bias=m.eps[0:NH, 1:2]).then_inc(gn_root, 1)

        @block.vector
        def _(dve):
            V = nc.vector
            link = Chain(dve, dch)

            def take(key, ins):
                ins.then_inc(by_dve, 1)

            ka = PAR_AT["rwkv_k_a"]
            link(V.tensor_scalar(omka, m.par[:, ka:ka + NP], -1.0, 1.0, ALU.mult, ALU.add))
            link(V.memset(keepmask, 1.0))
            link(V.memset(keepmask.rearrange("p (c t) -> p c t", c=NC)[:, :, 0:1], 0.0))
            for p in range(NP):
                wait_taken(dve, ("lora", p, "a"))
                V.tensor_tensor_scan(out=L[:, p, :], data0=keepmask, data1=L[:, p, :], initial=0.0, op0=ALU.mult,
                                     op1=ALU.add).then_inc(rate_ok, 1)
                dve.wait_ge(sq_ok, p + 1)
                link(V.tensor_scalar(tmp, a[:, p, :], par("rwkv_k_a", p), omka[:, p:p + 1], ALU.mult, ALU.add))
                link(V.tensor_tensor(zr[:, 4 + p, :], zr[:, 4 + p, :], tmp, ALU.mult))
            dve.wait_ge(up, n_up[("n2",)])
            V.tensor_scalar(norm, bk(("n2",))[0:NH, :], 1e-24, None, ALU.max).then_inc(n2_max, 1)
            dve.sem_inc(by_dve, 1)
            dve.wait_ge(n2_root, 1)
            V.reciprocal(norm, norm).then_inc(inverted, 1)
            for p in range(NP):
                dve.wait_ge(up, n_up[("inv", p)])
                take(("inv", p), V.tensor_tensor(kk[:, p, :], kk[:, p, :], bk(("inv", p))[:, :], ALU.mult))
            dve.wait_ge(by_dve, taken["dve"][("inv", NP - 1)])
            c3 = lambda x: x.rearrange("p (c t) -> p c t", c=NC)
            t3 = lambda x: x.rearrange("p (t n) -> p t n", t=NT)

            def vector_step(p, i):
                r, k = zr[:, p, :], zr[:, 4 + p, :]
                de = c3(Dd)[:, :, CH - 1:CH].to_broadcast([P, NC, CH])
                if i == 0:
                    link(V.tensor_tensor(a[:, p, :], a[:, p, :], kk[:, p, :], ALU.mult))
                elif i == 1:
                    dve.wait_ge(decay_ok, p + 1)
                    link(V.scalar_tensor_tensor(out=tmp, in0=k, scalar=par("rwkv_r_k", p), in1=r, op0=ALU.mult,
                                                op1=ALU.mult))
                elif i == 2:
                    link(V.tensor_tensor(c3(kk[:, p, :])[:, :, 1:CH], c3(kk[:, p, :])[:, :, 1:CH],
                                         c3(Dd)[:, :, 0:CH - 1], ALU.mult))
                elif i == 3:
                    link(V.tensor_tensor(r, r, Dd, ALU.mult))
                elif i == 4:
                    dve.wait_ge(inv_ok, p + 1)
                    link(V.tensor_tensor(k, k, L[:, p, :], ALU.mult))
                elif i == 5:
                    link(V.tensor_tensor(a[:, p, :], a[:, p, :], L[:, p, :], ALU.mult))
                elif i == 6:
                    V.tensor_tensor(c3(kapE), c3(k), de, ALU.mult)
                elif i == 7:
                    V.tensor_copy(m.dend.rearrange("p (j c) -> p j c", j=NP)[:, p, :].unsqueeze(2), c3(Dd)[:, :, CH - 1:CH])
                    V.tensor_tensor(c3(betaE), c3(a[:, p, :]), de, ALU.mult).then_inc(vec_ok, 1)

            for i in range(8):
                vector_step(0, i)
            for p in range(NP):
                v = zr[:, 8 + p, :]
                dve.wait_ge(up, n_up[("bonus", p)])
                take(("bonus", p), V.tensor_tensor(v, bk(("bonus", p))[:, :], v, ALU.mult))
                for n, dst, mask in (("LT", LT, m.strict), ("AK", AK, m.strict), ("RK", RK, m.incl), ("RB", None, m.incl)):
                    for hh in range(2):
                        dve.wait_ge(up, n_up[(n, p, hh)])
                        o = RB[:, 2 * p + hh, :] if dst is None else dst[:, hh, :]
                        take((n, p, hh), V.tensor_tensor(t3(o), t3(bk((n, p, hh))[:, :]),
                                                         mask.unsqueeze(1).to_broadcast([P, NT, P]), ALU.mult))
                for hh in range(2):
                    key = ("T", p, 1, hh)
                    dve.wait_ge(up, n_up[key])
                    take(key, V.tensor_tensor(t3(Tm[:, hh, :]), ident.unsqueeze(1).to_broadcast([P, NT, P]),
                                              t3(bk(key)[:, :]), ALU.subtract))
                for b in LEVELS[1:]:
                    first = 4 * LEVELS.index(b) - 8
                    for hh in range(2):
                        key = ("P", p, b, hh)
                        dve.wait_ge(up, n_up[key])
                        take(key, V.tensor_tensor(t3(Pm[:, hh, 0:NT * HALF]), t3(bk(key)[:, 0:NT * HALF]),
                                                  m.level[b].unsqueeze(1).to_broadcast([P, NT, HALF]), ALU.mult))
                        if p < NP - 1 and 0 <= first + hh < 8:
                            vector_step(p + 1, first + hh)
                    for hh in range(2):
                        key = ("T", p, b, hh)
                        dve.wait_ge(up, n_up[key])
                        x = firsts(Tm[:, hh, :], b)
                        take(key, V.tensor_tensor(x, x, bk(key)[:, 0:NT * HALF].rearrange(
                            "p (t n c) -> p t n c", t=NT, c=b), ALU.subtract))
                        if p < NP - 1 and 0 <= first + 2 + hh < 8:
                            vector_step(p + 1, first + 2 + hh)
                for i in range(2):
                    key = ("KV", p, i)
                    dve.wait_ge(up, n_up[key])
                    take(key, V.tensor_copy(KV[:, i:NC:2, p, :],
                                            bk(key)[:, 0:NT * HD].rearrange("p (c n) -> p c n", c=NT)))
            dve.wait_ge(by_act, len(taken["act"]))
            for c in range(NC):
                r, t = slice(CH * (c % 2), CH * (c % 2 + 1)), c // 2
                for hh in range(2):
                    dve.wait_ge(sa_up, 2 * c + hh + 1)
                    odd = lambda x: x[r, t, :].rearrange("p (j n) -> p j n", j=NP)[:, :, hh * HD:(hh + 1) * HD]
                    V.tensor_tensor(odd(nSA), bank[2 * (c % 2) + hh][r, 0:NP * HD].rearrange("p (j n) -> p j n", j=NP),
                                    odd(nU), ALU.add).then_inc(sa_ok, 1)
                dve.wait_ge(ds_up, c + 1)
                if c < NC - 1:
                    dve.wait_ge(base_ok, c + 1)
                    s = S[:, c + 1, :, :]
                    V.tensor_tensor(s, s, bank[4 + c % 2][:, 0:NP * HD].rearrange("p (j n) -> p j n", j=NP),
                                    ALU.add).then_inc(s_ok, 1)
                if c % 2 == 1:
                    dve.wait_ge(y_up, t + 1)
                    y = xT[:, NP:2 * NP, t * P:(t + 1) * P]
                    V.tensor_tensor(y, y, bank[6 + t % 2][:, :].rearrange("p (j n) -> p j n", j=NP),
                                    ALU.add).then_inc(y_ok, 1)
            for p in range(NP):
                y = xT[:, NP + p, :]
                dve.wait_ge(gn_up, p + 1)
                V.scalar_tensor_tensor(out=y, in0=bank[p % 2][:, :], scalar=-1.0 / HD, in1=y, op0=ALU.mult,
                                       op1=ALU.add).then_inc(gn_ctr, 1)
            for p in range(NP):
                y, v = xT[:, NP + p, :], zr[:, 8 + p, :]
                dve.wait_ge(gn_sq, p + 1)
                V.scalar_tensor_tensor(out=y, in0=y, scalar=par("rwkv_ln_w", p), in1=g[:, p, :], op0=ALU.mult, op1=ALU.mult)
                link(V.scalar_tensor_tensor(out=v, in0=v, scalar=par("rwkv_ln_b", p), in1=g[:, p, :], op0=ALU.add,
                                            op1=ALU.mult))
            dve.wait_ge(gn_root, 1)
            V.reciprocal(norm, norm).then_inc(inverted, 1)
            for p in range(NP):
                y = xT[:, NP + p, :]
                dve.wait_ge(gn_up, NP + 2 + p)
                V.tensor_tensor(y, y, bank[p % 2][:, :], ALU.mult).then_inc(scaled, 1)
                dve.wait_ge(scaled, p + 1)
                link(V.tensor_tensor(y, y, zr[:, 8 + p, :], ALU.add))


def route(nc, m, A):
    bank, ident, xT, h3, xh3 = m.bank, m.ident, m.xT, m.h3, m.xh3
    m.bias = m.misc[:, 3072:4608].bitcast(BF16)
    raw = m.misc[:, 0:3072]
    q = m.misc
    m.tabD = q[:, 4608:4808].rearrange("p (t b) -> p t b", t=NT)
    m.tabG = q[:, 4808:5008].rearrange("p (t b) -> p t b", t=NT)
    m.eint = q[:, 5008:5058].bitcast(I32)
    m.nint = q[:, 5058:5059].bitcast(I32)
    m.expert_is = q[:, 5060:5110]
    m.slots = q[:, 5112:5240]
    iotaB, iotaE, pmod = q[:, 5240:5290], q[:, 5290:5322], q[:, 5322:5323]
    rw = q[:, 5324:5580].rearrange("p (k e) -> p k e", k=KD)
    w = m.w[:, 16384:24576]
    before, ones, rb = w[:, 0:128], w[:, 128:256], w[:, 256:288]
    lg = w[:, 512:640].rearrange("p (t e) -> p t e", t=NT)
    top = w[:, 640:672].rearrange("p (t k) -> p t k", t=NT)
    topi = w[:, 672:704].bitcast(U32).rearrange("p (t k) -> p t k", t=NT)
    topf = w[:, 704:736].rearrange("p (t k) -> p t k", t=NT)
    gate = w[:, 736:752].rearrange("p (t k) -> p t k", t=NT)
    gsum, nv0 = w[:, 752:756], w[:, 756:760]
    OH = w[:, 1024:1536].rearrange("p (t k e) -> p t k e", t=NT, k=TOPE)
    prod = w[:, 1536:2048].rearrange("p (t k e) -> p t k e", t=NT, k=TOPE)
    M = w[:, 2048:2176].rearrange("p (t e) -> p t e", t=NT)
    fl = w[:, 2176:2304].rearrange("p (t e) -> p t e", t=NT)
    slot = w[:, 2304:2432].rearrange("p (t e) -> p t e", t=NT)
    blk = w[:, 2432:2560].rearrange("p (t e) -> p t e", t=NT)
    tmp = w[:, 2560:2688].rearrange("p (t e) -> p t e", t=NT)
    nb, bend, bstart = w[:, 2688:2720], w[:, 2720:2752], w[:, 2752:2784]
    blk_k = w[:, 2784:2800].rearrange("p (t k) -> p t k", t=NT)
    slot_k = w[:, 2800:2816].rearrange("p (t k) -> p t k", t=NT)
    eq = w[:, 4992:5792].rearrange("p (t b k) -> p t b k", t=NT, k=TOPE)
    eq2 = w[:, 5792:6592].rearrange("p (t b k) -> p t b k", t=NT, k=TOPE)
    le = w[:, 3216:3216 + NBT * NE].rearrange("p (b e) -> p b e", b=NBT)
    ef = w[:, 4864:4864 + NBT]
    sem = m.sem
    out_up, h_ok, ss_ok, var_ok, root_ok, xh_ok, x_up = (sem(n) for n in (
        "out_up", "h_ready", "h_squared", "h_var", "h_root", "h_normed", "h_transposed"))
    xa, xv, lg_up, rank_up, m_ok = (sem(n) for n in ("hT_by_act", "hT_by_dve", "router_up", "ranks_up", "choice_ready"))
    rb_in, iota_ok, v0_ok, g_ok = sem("router_loaded"), sem("iota_ready"), sem("top_ready"), sem("gates_up")
    bias_in, dch, pch = sem("bias_loaded"), sem("route_dve_step"), sem("route_pool_step")
    m.raw_in = [sem(f"weights_loaded{k}") for k in range(4)]
    m.raw4 = m.raw[:, :].rearrange("p (k n) -> p k n", k=4)
    m.gu_dram = A["exp_w_gu"][0].rearrange("e (k p) n -> e p k n", p=P)
    n2row, n2_in = w[:, 6656:7680], sem("norm2_row_loaded")
    xn_ok, hi_ok = sem("xn_ready"), sem("xn_hi_ready")
    xn_hi = m.xn_hi[:, :].rearrange("p (t d) -> p t d", t=NT)
    xn_lo = m.xn_lo[:, :].rearrange("p (t d) -> p t d", t=NT)
    with nc.Block() as block:
        @block.sync
        def _(sp):
            sp.dma_start(rw, A["router_w"][0].rearrange("(k p) e -> p k e", p=P)).then_inc(rb_in, 16)
            sp.dma_start(rb, A["router_b"][0].partition_broadcast(P)).then_inc(rb_in, 16)
            for r in range(3):
                sp.dma_start(raw[NE * r:NE * (r + 1), 0:2 * FF], A["exp_b_gu"][0]).then_inc(bias_in, 16)
                sp.dma_start(raw[NE * r:NE * (r + 1), 2 * FF:3 * FF], A["exp_b_down"][0]).then_inc(bias_in, 16)
            sp.dma_start(n2row, A["norm2_w"][0].partition_broadcast(P)).then_inc(n2_in, 16)
            for k in range(4):
                sp.dma_start(m.raw4[:, k, :], m.gu_dram[0, :, k, :]).then_inc(m.raw_in[k], 16)

        @block.gpsimd
        def _(pool):
            G = nc.gpsimd
            link = Chain(pool, pch)
            G.iota(m.slots, [[1, P]], base=0, channel_multiplier=0, allow_small_or_imprecise_dtypes=True)
            G.iota(iotaB, [[1, NBT]], base=-1, channel_multiplier=0, allow_small_or_imprecise_dtypes=True)
            G.iota(iotaE, [[1, NE]], base=0, channel_multiplier=0, allow_small_or_imprecise_dtypes=True)
            link(G.iota(pmod, [[0, 1]], base=0, channel_multiplier=1, allow_small_or_imprecise_dtypes=True))
            link(G.tensor_scalar(pmod[32:64, :], pmod[32:64, :], -32.0, None, ALU.add))
            link(G.tensor_scalar(pmod[64:96, :], pmod[64:96, :], -64.0, None, ALU.add))
            link(G.memset(before, 1.0))
            link(G.memset(ones, 1.0))
            G.affine_select(out=before, in_=before, compare_op=ALU.is_gt, fill=0.0, base=0, pattern=[[1, P]],
                            channel_multiplier=-1).then_inc(iota_ok, 1)
            pool.wait_ge(bias_in, 96)
            link(G.tensor_copy(m.bias[0:96, :], raw[0:96, :]))
            for lo, hi in ((32, 64), (64, 96)):
                link(G.tensor_tensor(raw[lo:hi, :], raw[lo:hi, :], m.bias[lo:hi, :], ALU.subtract))
                link(G.tensor_copy(m.bias[lo:hi, :], raw[lo:hi, :]))
            link(G.tensor_tensor(raw[64:96, :], raw[64:96, :], m.bias[64:96, :], ALU.subtract))
            link(G.tensor_copy(m.bias[64:96, :], raw[64:96, :]))

        @block.tensor
        def _(pe):
            MM = nc.tensor.matmul
            for g in range(2 * NT):
                out_group(nc, m, g, range(NP if g < 6 else 0, KD)).then_inc(out_up, 1)
            pe.wait_ge(h_ok, 2 * NT)
            for t in range(NT):
                pe.wait_ge(xh_ok, t + 1)
                for k in range(KD):
                    mm = nc.tensor.transpose(bank[k][:, t * P:(t + 1) * P], xh3[:, t, k * P:(k + 1) * P], ident)
            mm.then_inc(x_up, 1)
            pe.wait_ge(xa, KD // 2)
            pe.wait_ge(xv, KD // 2)
            pe.wait_ge(rb_in, 32)
            for t in range(NT):
                for k in range(KD):
                    mm = MM(bank[0][:, t * NE:(t + 1) * NE], xT[:, k, t * P:(t + 1) * P], rw[:, k, :],
                            start=(k == 0), stop=(k == KD - 1))
            mm.then_inc(lg_up, 1)
            pe.wait_ge(iota_ok, 1)
            pe.wait_ge(m_ok, 1)
            for t in range(NT):
                for s in range(t + 1):
                    MM(bank[1][:, t * NE:(t + 1) * NE], before if s == t else ones, M[:, s, :], start=(s == 0), stop=(s == t))
            for t in range(NT):
                mm = MM(bank[1][:, NT * NE:(NT + 1) * NE], ones, M[:, t, :], start=(t == 0), stop=(t == NT - 1))
            mm.then_inc(rank_up, 1)

        @block.scalar
        def _(act):
            for t in range(NT):
                act.wait_ge(h_ok, 2 * (t + 1))
                nc.scalar.activation(xh3[:, t, :], h3[:, t, :], ACT.Square, accum_out=m.ss[:, t:t + 1]).then_inc(ss_ok, 1)
            act.wait_ge(var_ok, 1)
            nc.scalar.activation(m.rstd, m.ss, ACT.Sqrt).then_inc(root_ok, 1)
            act.wait_ge(x_up, 1)
            n2 = PAR_AT["norm2_w"]
            for k in range(0, KD, 2):
                nc.scalar.activation(xT[:, k, :], bank[k][:, :], ACT.Copy, scale=m.par[:, n2 + k:n2 + k + 1]).then_inc(xa, 1)
            for t in range(NT):
                act.wait_ge(xn_ok, t + 1)
                nc.scalar.activation(xn_hi[:, t, :], xh3[:, t, :], ACT.Copy).then_inc(hi_ok, 1)
            act.wait_ge(v0_ok, 1)
            for t in range(NT):
                a = nc.scalar.activation(gate[:, t, :], top[:, t, 0:TOPE], ACT.Exp, bias=nv0[:, t:t + 1],
                                         accum_out=gsum[:, t:t + 1])
                a.then_inc(g_ok, 1)

        @block.vector
        def _(dve):
            V = nc.vector
            link = Chain(dve, dch)
            for t in range(NT):
                for half in range(2):
                    dve.wait_ge(out_up, 2 * t + half + 1)
                    hh = h3[:, t, half * 512:(half + 1) * 512]
                    V.tensor_tensor(hh, hh, out_bank(m, 2 * t + half)[:, :], ALU.add).then_inc(h_ok, 1)
            dve.wait_ge(ss_ok, NT)
            V.tensor_scalar(m.ss, m.ss, 1.0 / D, RMS_EPS, ALU.mult, ALU.add).then_inc(var_ok, 1)
            dve.wait_ge(root_ok, 1)
            link(V.reciprocal(m.rstd, m.rstd))
            for t in range(NT):
                V.tensor_scalar(xh3[:, t, :], h3[:, t, :], m.rstd[:, t:t + 1], None, ALU.mult).then_inc(xh_ok, 1)
            dve.wait_ge(x_up, 1)
            n2 = PAR_AT["norm2_w"]
            for k in range(1, KD, 2):
                V.tensor_scalar(xT[:, k, :], bank[k][:, :], m.par[:, n2 + k:n2 + k + 1], None, ALU.mult).then_inc(xv, 1)
            dve.wait_ge(n2_in, 16)
            for t in range(NT):
                V.tensor_tensor(xh3[:, t, :], xh3[:, t, :], n2row, ALU.mult).then_inc(xn_ok, 1)
            for t in range(NT):
                dve.wait_ge(hi_ok, t + 1)
                V.tensor_tensor(xn_lo[:, t, :], xh3[:, t, :], xn_hi[:, t, :].bitcast(F32), ALU.subtract)
            dve.wait_ge(lg_up, 1)
            dve.wait_ge(rb_in, 32)
            link(V.tensor_tensor(lg, bank[0][:, 0:NT * NE].rearrange("p (t e) -> p t e", t=NT),
                                 rb.unsqueeze(1).to_broadcast([P, NT, NE]), ALU.add))
            for t in range(NT):
                link(V.max(out=top[:, t, :], in_=lg[:, t, :]))
                link(V.max_index(out=topi[:, t, :], in_max=top[:, t, :], in_values=lg[:, t, :]))
            V.tensor_scalar(nv0, top[:, :, 0], -1.0, None, ALU.mult).then_inc(v0_ok, 1)
            link(V.tensor_copy(topf, topi))
            dve.wait_ge(iota_ok, 1)
            shape = [P, NT, TOPE, NE]
            link(V.tensor_tensor(OH, iotaE.unsqueeze(1).unsqueeze(1).to_broadcast(shape),
                                 topf[:, :, 0:TOPE].unsqueeze(3).to_broadcast(shape), ALU.is_equal))
            V.tensor_reduce(M, OH.rearrange("p t k e -> p t e k"), AX.X, ALU.add).then_inc(m_ok, 1)
            dve.wait_ge(g_ok, NT)
            link(V.reciprocal(gsum, gsum))
            link(V.tensor_tensor(gate, gate, gsum.unsqueeze(2).to_broadcast([P, NT, TOPE]), ALU.mult))
            dve.wait_ge(rank_up, 1)
            cnt = bank[1][:, NT * NE:(NT + 1) * NE]
            rank = bank[1][:, 0:NT * NE].rearrange("p (t e) -> p t e", t=NT)
            link(V.tensor_scalar(nb, cnt, float(P), 1.0, ALU.is_gt, ALU.add))
            for x in (2, 3):
                link(V.tensor_scalar(bstart, cnt, float(x * P), None, ALU.is_gt))
                link(V.tensor_tensor(nb, nb, bstart, ALU.add))
            link(V.tensor_tensor_scan(out=bend, data0=ones[:, 0:NE], data1=nb, initial=0.0, op0=ALU.mult, op1=ALU.add))
            link(V.tensor_tensor(bstart, bend, nb, ALU.subtract))
            link(V.tensor_scalar(fl, rank, float(P), None, ALU.is_ge))
            for x in (2, 3):
                link(V.tensor_scalar(tmp, rank, float(x * P), None, ALU.is_ge))
                link(V.tensor_tensor(fl, fl, tmp, ALU.add))
            link(V.scalar_tensor_tensor(out=slot, in0=fl, scalar=-float(P), in1=rank, op0=ALU.mult, op1=ALU.add))
            link(V.tensor_scalar(slot, slot, 1.0, None, ALU.add))
            link(V.tensor_tensor(blk, fl, bstart.unsqueeze(1).to_broadcast([P, NT, NE]), ALU.add))
            for src, dst in ((blk, blk_k), (slot, slot_k)):
                link(V.tensor_tensor(prod, OH, src.unsqueeze(2).to_broadcast(shape), ALU.mult))
                link(V.tensor_reduce(dst, prod, AX.X, ALU.add))
            tb = [P, NT, NBT, TOPE]
            link(V.tensor_tensor(eq, iotaB.unsqueeze(1).unsqueeze(3).to_broadcast(tb),
                                 blk_k.unsqueeze(2).to_broadcast(tb), ALU.is_equal))
            for src, tab in ((slot_k, m.tabD), (gate, m.tabG)):
                link(V.tensor_tensor(eq2, eq, src.unsqueeze(2).to_broadcast(tb), ALU.mult))
                link(V.tensor_reduce(tab, eq2, AX.X, ALU.add))
            link(V.tensor_scalar(m.tabD, m.tabD, -1.0, None, ALU.add))
            be = [P, NBT, NE]
            link(V.tensor_tensor(le, bend.unsqueeze(1).to_broadcast(be), iotaB.unsqueeze(2).to_broadcast(be), ALU.is_le))
            link(V.tensor_reduce(ef, le, AX.X, ALU.add))
            link(V.tensor_scalar(ef, ef, float(NE - 1), None, ALU.min))
            link(V.tensor_copy(m.eint, ef))
            link(V.tensor_copy(m.nint, bend[:, NE - 1:NE]))
            link(V.tensor_scalar(m.expert_is, ef, pmod, None, ALU.is_equal))


def experts(nc, m, A, out):
    bank, ident, h3, raw4 = m.bank, m.ident, m.h3, m.raw4
    NS = 12
    w_hi = m.w_hi[:, :].rearrange("p (k n) -> p k n", k=4)
    w_lo = m.w_lo[:, :].rearrange("p (k n) -> p k n", k=4)
    xn = [x[:, :].rearrange("p (t d) -> p t d", t=NT) for x in (m.xn_hi, m.xn_lo)]
    r = m.parts
    xg = [r[:, 1024 * i:1024 * (i + 1)].rearrange("p (k s) -> p k s", k=KD) for i in (0, 1)]
    actT = [r[:, 1024 * i:1024 * (i + 1)].rearrange("p (k s) -> p k s", k=KD) for i in (2, 3)]
    yb = [r[:, 1024 * i:1024 * (i + 1)] for i in (4, 5)]
    pick = r[:, 6144:6656].rearrange("p (t s) -> p t s", t=NT)
    place = r[:, 6656:7168].rearrange("p (t s) -> p t s", t=NT)
    glu, lin, sig = (m.misc[:, 1024 * i:1024 * (i + 1)] for i in range(3))
    who = m.con[:, P:P + P // 2].bitcast(BF16)
    rows = m.con[:, 3 * P:3 * P + D]
    gcol, dcol = m.con[:, 2 * P:2 * P + NT], m.con[:, 2 * P + 8:2 * P + 8 + NT]
    dn_dram = A["exp_w_down"][0].rearrange("e (k p) n -> e p k n", p=P)
    out3 = out[0].rearrange("(t p) d -> p t d", p=P)
    sem = m.sem
    hi_ok, lo_ok, w_used = sem("weights_hi_ready"), sem("weights_lo_ready"), sem("weights_used")
    ready = sem("moe_cleared")
    pick_ok, place_up, place_ok, who_ok = sem("pick_ready"), sem("place_up"), sem("place_ready"), sem("who_ready")
    xg_up, xg_ok, xgT_up = sem("gathered_up"), sem("gathered_ready"), sem("gatheredT_up")
    xgT_hi, xgT_lo, h_up = sem("gatheredT_hi_ready"), sem("gatheredT_lo_ready"), sem("hidden_up")
    glu_ok, sig_ok, lin_ok, mid_ok, act_ok, actT_up, hiT_ok, loT_ok = (sem(n) for n in (
        "glu_ready", "sigmoid_ready", "linear_ready", "linear_times_glu_ready", "activation_ready", "actT_up",
        "actT_hi_ready", "actT_lo_ready"))
    y_up, yhi_ok, ylo_ok, add_up, add_ok, stored = (sem(n) for n in (
        "expert_out_up", "out_hi_ready", "out_lo_ready", "scattered_up", "scattered_added", "output_stored"))
    col_ok = sem("columns_ready")
    nblocks = dict(min_val=NE, max_val=MAXB - 1)

    def source(e, s):
        v = m.gu_dram[bass.ds(e, 1), :, s, :] if s < KD else dn_dram[bass.ds(e, 1), :, 2 * (s - KD):2 * (s - KD) + 2, :]
        return v.squeeze(0)

    def raw_slice(s):
        v = raw4[:, s % 4, :]
        return v if s < KD else v.rearrange("p (k n) -> p k n", k=2)

    with nc.Block() as block:
        @block.sync
        def _(sp):
            n = sp.value_load(m.nint[0:1, 0:1], **nblocks)
            with sp.Fori(0, n) as b:
                for s in range(4, NS + 4):
                    if s == 4 or s == NS:
                        e = sp.value_load(m.eint[0:1, bass.ds(b + (1 + s // NS), 1)], min_val=0, max_val=NE - 1)
                    sp.wait_ge(hi_ok, b * NS + (s - 3))
                    sp.wait_ge(lo_ok, b * NS + (s - 3))
                    sp.dma_start(raw_slice(s % NS), source(e, s % NS)).then_inc(m.raw_in[s % 4], 16)
            for q in range(4):
                sp.wait_ge(m.raw_in[q], n * 48 + 16)
            for t in range(NT):
                sp.wait_ge(add_ok, n * (2 * NT) + 2 * (t + 1))
                sp.dma_start(out3[:, t, :], h3[:, t, :]).then_inc(stored, 16)
            sp.wait_ge(stored, 16 * NT)

        @block.gpsimd
        def _(pool):
            nc.gpsimd.memset(place.bitcast(F32), 0.0)
            nc.gpsimd.memset(yb[0].bitcast(F32), 0.0)
            nc.gpsimd.memset(yb[1].bitcast(F32), 0.0).then_inc(ready, 1)

        @block.tensor
        def _(pe):
            MM = nc.tensor.matmul
            n = pe.value_load(m.nint[0:1, 0:1], **nblocks)

            def gather(half):
                c = slice(half * 512, (half + 1) * 512)
                for part in (0, 1):
                    for t in range(NT):
                        mm = MM(bank[4 + half][:, :], pick[:, t, :], xn[part][:, t, c],
                                start=(part == 0 and t == 0), stop=(part == 1 and t == NT - 1))
                mm.then_inc(xg_up, 1)

            def turn_rows(before):
                for half in (1, 0):
                    pe.wait_ge(xg_ok, before + (2 - half))
                    for q in range(4):
                        mm = nc.tensor.transpose(bank[3 - half][:, q * P:(q + 1) * P],
                                                 rows[:, (4 * half + q) * P:(4 * half + q + 1) * P], ident)
                    mm.then_inc(xgT_up, 1)

            def turn_activation(i, before):
                pe.wait_ge(act_ok, before + (i + 1))
                for q in range(4):
                    k = 4 * i + q
                    mm = nc.tensor.transpose(bank[i][:, q * P:(q + 1) * P], glu[:, k * P:(k + 1) * P], ident)
                mm.then_inc(actT_up, 1)

            def scatter(i, before):
                if i >= 2:
                    pe.wait_ge(add_ok, before + (i - 1))
                c = slice((i % 2) * 512, (i % 2 + 1) * 512)
                MM(bank[6 + i % 2][:, :], place[:, i // 2, :], yb[0][:, c], start=True, stop=False)
                MM(bank[6 + i % 2][:, :], place[:, i // 2, :], yb[1][:, c], start=False, stop=True).then_inc(add_up, 1)

            def passes(outs, stationary, w, c0, q, first=False):
                for j, o in enumerate(outs):
                    mm = MM(o[:, :], stationary, w[:, q, c0 + j * 512:c0 + (j + 1) * 512], start=first, stop=False)
                return mm

            def three(outs, stationary, k0, s, before):
                n = 512 * len(outs)
                tiles = [(k0 + u, u * n) for u in range(2048 // n)]
                pe.wait_ge(hi_ok, before + (s + 1))
                for k, c in tiles:
                    passes(outs, stationary[0][:, k, :], w_hi, c, s % 4, first=(k == 0))
                    passes(outs, stationary[1][:, k, :], w_hi, c, s % 4)
                pe.wait_ge(lo_ok, before + (s + 1))
                for k, c in tiles:
                    mm = passes(outs, stationary[0][:, k, :], w_lo, c, s % 4)
                mm.then_inc(w_used, 1)

            def add_bias(o, j):
                return MM(o[:, :], who[0:96, :], m.bias[0:96, j * 512:(j + 1) * 512], start=False, stop=True)

            pe.sem_inc(w_used, 4)
            pe.wait_ge(pick_ok, 1)
            gather(1)
            gather(0)
            turn_rows(0)
            pe.wait_ge(ready, 1)
            with pe.Fori(0, n) as b:
                pe.wait_ge(xgT_hi, b * 2 + 2)
                pe.wait_ge(xgT_lo, b * 2 + 2)
                for s in range(KD):
                    three(bank[0:4], xg, s, s, b * NS)
                    if s == 1:
                        pe.wait_ge(yhi_ok, b * 2 + 2)
                        pe.wait_ge(ylo_ok, b * 2 + 2)
                        pe.wait_ge(place_ok, b + 1)
                    if 1 <= s <= 3:
                        scatter(2 * (s - 1), b * (2 * NT))
                        scatter(2 * (s - 1) + 1, b * (2 * NT))
                    if s == 5:
                        for t in range(NT):
                            mm = nc.tensor.transpose(bank[4][:, t * P:(t + 1) * P], pick[:, t, :].bitcast(F32), ident)
                        mm.then_inc(place_up, 1)
                pe.wait_ge(who_ok, b + 1)
                for j in (0, 2, 1, 3):
                    add_bias(bank[j], j).then_inc(h_up, 1)
                scatter(6, b * (2 * NT))
                scatter(7, b * (2 * NT))
                pe.wait_ge(pick_ok, b + 2)
                gather(1)
                turn_activation(0, b * 2)
                pe.wait_ge(place_ok, b + 2)
                gather(0)
                turn_activation(1, b * 2)
                turn_rows(b * 2 + 2)
                for s in range(KD, NS):
                    i = (s - KD) // 2
                    if s % 2 == 0:
                        pe.wait_ge(hiT_ok, b * 2 + (i + 1))
                        pe.wait_ge(loT_ok, b * 2 + (i + 1))
                    three(bank[4:6], actT, 2 * (s - KD), s, b * NS)
                pe.wait_ge(add_ok, b * (2 * NT) + 2 * NT)
                for j in range(2):
                    add_bias(bank[4 + j], 4 + j).then_inc(y_up, 1)
            pe.wait_ge(yhi_ok, n * 2 + 2)
            pe.wait_ge(ylo_ok, n * 2 + 2)
            pe.wait_ge(place_ok, n + 1)
            for i in range(2 * NT):
                scatter(i, n * (2 * NT))

        @block.scalar
        def _(act):
            C = nc.scalar.activation
            n = act.value_load(m.nint[0:1, 0:1], **nblocks)

            def high_part(s, before):
                act.wait_ge(m.raw_in[s % 4], before * 4 + 16 * (s // 4 + 1))
                act.wait_ge(w_used, before + (s + 1))
                C(w_hi[:, s % 4, :], raw4[:, s % 4, :], ACT.Copy).then_inc(hi_ok, 1)

            def keep_rows(half, before):
                act.wait_ge(xg_up, before + (2 - half))
                C(rows[:, half * 512:(half + 1) * 512], bank[4 + half][:, :], ACT.Copy).then_inc(xg_ok, 1)

            def keep_activation(i, before):
                act.wait_ge(actT_up, before + (i + 1))
                C(actT[0][:, 4 * i:4 * i + 4, :], bank[i][:, :].rearrange("p (k s) -> p k s", k=4),
                  ACT.Copy).then_inc(hiT_ok, 1)

            def keep_turned(before):
                for i, half in enumerate((1, 0)):
                    act.wait_ge(xgT_up, before + (i + 1))
                    C(xg[0][:, 4 * half:4 * half + 4, :], bank[3 - half][:, :].rearrange("p (k s) -> p k s", k=4),
                      ACT.Copy).then_inc(xgT_hi, 1)

            def sigmoid(i, before):
                act.wait_ge(glu_ok, before + (i + 1))
                c = slice(i * 512, (i + 1) * 512)
                C(sig[:, c], glu[:, c], ACT.Sigmoid, scale=ALPHA).then_inc(sig_ok, 1)

            act.wait_ge(ready, 1)
            act.sem_inc(yhi_ok, 2)
            act.sem_inc(place_ok, 1)
            keep_rows(1, 0)
            keep_rows(0, 0)
            keep_turned(0)
            for s in range(4):
                high_part(s, 0)
            with act.Fori(0, n) as b:
                C(m.nmx[:, 0:1], m.eps[:, 0:1], ACT.Sigmoid)
                for s in range(4, NS):
                    high_part(s, b * NS)
                sigmoid(0, b * 2)
                act.wait_ge(place_up, b + 1)
                act.wait_ge(add_up, b * (2 * NT) + 2 * NT)
                C(place, bank[4][:, :].rearrange("p (t s) -> p t s", t=NT), ACT.Copy).then_inc(place_ok, 1)
                sigmoid(1, b * 2)
                keep_rows(1, b * 2 + 2)
                keep_activation(0, b * 2)
                keep_rows(0, b * 2 + 2)
                keep_activation(1, b * 2)
                keep_turned(b * 2 + 2)
                for s in range(4):
                    high_part(s, b * NS + NS)
                for j in range(2):
                    act.wait_ge(y_up, b * 2 + (j + 1))
                    C(yb[0][:, j * 512:(j + 1) * 512], bank[4 + j][:, :], ACT.Copy).then_inc(yhi_ok, 1)

        @block.vector
        def _(dve):
            V = nc.vector
            n = dve.value_load(m.nint[0:1, 0:1], **nblocks)

            def low_part(s, before):
                dve.wait_ge(hi_ok, before + (s + 1))
                V.tensor_tensor(w_lo[:, s % 4, :], raw4[:, s % 4, :], w_hi[:, s % 4, :].bitcast(F32),
                                ALU.subtract).then_inc(lo_ok, 1)

            def split_turned(before):
                for i, half in enumerate((1, 0)):
                    dve.wait_ge(xgT_hi, before + (i + 1))
                    h = slice(4 * half, 4 * half + 4)
                    V.tensor_tensor(xg[1][:, h, :], bank[3 - half][:, :].rearrange("p (k s) -> p k s", k=4),
                                    xg[0][:, h, :].bitcast(F32), ALU.subtract).then_inc(xgT_lo, 1)

            def build_pick():
                shape = [P, NT, P]
                V.tensor_tensor(pick, m.slots.unsqueeze(1).to_broadcast(shape), dcol.unsqueeze(2).to_broadcast(shape),
                                ALU.is_equal).then_inc(pick_ok, 1)

            def add(i, before):
                dve.wait_ge(add_up, before + (i + 1))
                hh = h3[:, i // 2, (i % 2) * 512:(i % 2 + 1) * 512]
                V.scalar_tensor_tensor(out=hh, in0=bank[6 + i % 2][:, :], scalar=gcol[:, i // 2:i // 2 + 1], in1=hh,
                                       op0=ALU.mult, op1=ALU.add).then_inc(add_ok, 1)

            V.tensor_copy(dcol, m.tabD[:, :, 1]).then_inc(col_ok, 1)
            dve.wait_ge(ready, 1)
            dve.sem_inc(ylo_ok, 2)
            dve.wait_ge(col_ok, 1)
            build_pick()
            split_turned(0)
            for s in range(4):
                low_part(s, 0)
            with dve.Fori(0, n) as b:
                dve.wait_ge(pick_ok, b + 1)
                dve.wait_ge(ylo_ok, b * 2 + 2)
                V.tensor_copy(gcol.unsqueeze(2), m.tabG[:, :, bass.ds(b, 1)])
                V.tensor_copy(dcol.unsqueeze(2), m.tabD[:, :, bass.ds(b + 2, 1)]).then_inc(col_ok, 1)
                dve.wait_ge(col_ok, b + 2)
                for s in range(4, NS - 2):
                    low_part(s, b * NS)
                    if s <= 6:
                        add(2 * (s - 4), b * (2 * NT))
                        add(2 * (s - 4) + 1, b * (2 * NT))
                    if s == 9:
                        dve.wait_ge(place_up, b + 1)
                        V.tensor_copy(who[0:96, :], m.expert_is[0:96, bass.ds(b + 1, 1)].to_broadcast([96, P]))\
                            .then_inc(who_ok, 1)
                        build_pick()
                half = [slice(i * 512, (i + 1) * 512) for i in range(2)]

                def clip_glu(i):
                    dve.wait_ge(h_up, b * 4 + (2 * i + 1))
                    V.tensor_scalar(glu[:, half[i]], bank[i][:, :], LIMIT, None, ALU.min).then_inc(glu_ok, 1)

                def clip_linear(i):
                    dve.wait_ge(h_up, b * 4 + (2 * i + 2))
                    V.tensor_scalar(lin[:, half[i]], bank[2 + i][:, :], LIMIT, -LIMIT, ALU.min, ALU.max).then_inc(lin_ok, 1)
                    dve.wait_ge(glu_ok, b * 2 + (i + 1))
                    dve.wait_ge(lin_ok, b * 2 + (i + 1))
                    V.scalar_tensor_tensor(out=lin[:, half[i]], in0=lin[:, half[i]], scalar=1.0, in1=glu[:, half[i]],
                                           op0=ALU.add, op1=ALU.mult).then_inc(mid_ok, 1)

                def activation(i):
                    dve.wait_ge(mid_ok, b * 2 + (i + 1))
                    dve.wait_ge(sig_ok, b * 2 + (i + 1))
                    V.tensor_tensor(glu[:, half[i]], lin[:, half[i]], sig[:, half[i]], ALU.mult).then_inc(act_ok, 1)

                def split_activation(i):
                    dve.wait_ge(hiT_ok, b * 2 + (i + 1))
                    V.tensor_tensor(actT[1][:, 4 * i:4 * i + 4, :], bank[i][:, :].rearrange("p (k s) -> p k s", k=4),
                                    actT[0][:, 4 * i:4 * i + 4, :].bitcast(F32), ALU.subtract).then_inc(loT_ok, 1)

                clip_glu(0)
                clip_linear(0)
                clip_glu(1)
                activation(0)
                clip_linear(1)
                activation(1)
                split_activation(0)
                add(6, b * (2 * NT))
                split_activation(1)
                add(7, b * (2 * NT))
                low_part(NS - 2, b * NS)
                low_part(NS - 1, b * NS)
                split_turned(b * 2 + 2)
                for s in range(4):
                    low_part(s, b * NS + NS)
                for j in range(2):
                    dve.wait_ge(yhi_ok, b * 2 + (j + 3))
                    V.tensor_tensor(yb[1][:, j * 512:(j + 1) * 512], bank[4 + j][:, :],
                                    yb[0][:, j * 512:(j + 1) * 512].bitcast(F32), ALU.subtract).then_inc(ylo_ok, 1)
            dve.wait_ge(ylo_ok, n * 2 + 2)
            V.tensor_copy(gcol.unsqueeze(2), m.tabG[:, :, bass.ds(n, 1)]).then_inc(col_ok, 1)
            dve.wait_ge(col_ok, n + 2)
            for i in range(2 * NT):
                add(i, n * (2 * NT))


def build(nc, A, out):
    with ExitStack() as ctx:
        m = memory(nc, ctx)
        constants(nc, m, A)
        project(nc, m, A)
        attention(nc, m, A)
        rwkv(nc, m, A)
        route(nc, m, A)
        experts(nc, m, A, out)


_INS = ["x", "positions", "norm1_w", "w_in", "q_norm_w", "k_norm_w", "rwkv_mu", "rwkv_w0", "rwkv_w2", "rwkv_a0",
        "rwkv_a2", "rwkv_g2", "rwkv_k_k", "rwkv_k_a", "rwkv_r_k", "rwkv_ln_w", "rwkv_ln_b", "w_out", "norm2_w",
        "router_w", "router_b", "exp_w_gu", "exp_b_gu", "exp_w_down", "exp_b_down"]


def kernel(**inputs):
    import concourse.bacc as _bacc
    from concourse.bass_utils import run_bass_kernel_spmd as _run

    nc = _bacc.Bacc("TRN2", target_bir_lowering=False, num_devices=1)
    arrays, args = {}, {}
    for name in _INS:
        a = np.ascontiguousarray(inputs[name])
        arrays[f"in_{name}"] = a
        args[name] = nc.dram_tensor(f"in_{name}", a.shape, mybir.dt.from_np(a.dtype), kind="ExternalInput").ap()
    out = nc.dram_tensor("out_0", (1, T, D), F32, kind="ExternalOutput").ap()
    build(nc, args, out)
    return _run(nc, [arrays], core_ids=[0]).results[0]["out_0"]
```
